# Optimizing a Trainium2 kernel written in Bass

```python
import jax, jax.numpy as jnp
from jax import lax
import numpy as np

D_MODEL = 1024
BATCH = 1
SEQ = 1024
DEPTH = 1

HEAD_DIM = 64
N_HEADS_NSA = 8
N_KV_NSA = 2
GROUP = N_HEADS_NSA // N_KV_NSA
N_HEADS_FOX = 8
D_NSA = N_HEADS_NSA * HEAD_DIM
D_KV_NSA = N_KV_NSA * HEAD_DIM
D_FOX = N_HEADS_FOX * HEAD_DIM
CMP_BLOCK = 32
CMP_STRIDE = 16
CMP_RATIO = CMP_BLOCK // CMP_STRIDE
CMP_HIDDEN = 128
SLC_BLOCK = 64
TOP_N = 16
WINDOW = 512
NSA_Q_BLOCK = 64
Q_BLOCK = 128
ROPE_THETA = 500000.0
ROPE_DIM = HEAD_DIM // 4
D_FF = 2816
N_MOD = 9
RMS_EPS = 1e-6
NEG_INF = -1e30
FORCE_SCORE = 1e4
IN_SIZES = (D_NSA, D_KV_NSA, D_KV_NSA, D_KV_NSA, D_KV_NSA, D_KV_NSA, D_KV_NSA,
            3 * N_HEADS_NSA, D_FOX, D_FOX, D_FOX, N_HEADS_FOX, D_MODEL, D_MODEL)
D_IN = sum(IN_SIZES)

kernel_name = "macaron_nsa_fox_hybrid_adaln"

def rms_norm(x, g):
    xf = x.astype(jnp.float32)
    y = xf * lax.rsqrt(jnp.mean(xf * xf, axis=-1, keepdims=True) + RMS_EPS)
    return (y * g.astype(jnp.float32)).astype(x.dtype)

def modulate(h, shift, scale):
    return h * (1 + scale[:, None, :]) + shift[:, None, :]

def swiglu(h, w_gate, w_up, w_down):
    return (jax.nn.silu(h @ w_gate) * (h @ w_up)) @ w_down

def partial_rope(x, positions):
    half = ROPE_DIM // 2
    inv_freq = ROPE_THETA ** (-jnp.arange(half, dtype=jnp.float32) / half)
    ang = positions.astype(jnp.float32)[..., None] * inv_freq
    cos = jnp.cos(ang)[:, :, None, :]
    sin = jnp.sin(ang)[:, :, None, :]
    xr = x[..., :ROPE_DIM].astype(jnp.float32)
    x1, x2 = xr[..., :half], xr[..., half:]
    rot = jnp.concatenate([x1 * cos - x2 * sin, x2 * cos + x1 * sin], axis=-1).astype(x.dtype)
    return jnp.concatenate([rot, x[..., ROPE_DIM:]], axis=-1)

def masked_softmax(s, mask):
    p = jax.nn.softmax(jnp.where(mask, s, NEG_INF), axis=-1)
    return jnp.where(mask, p, 0.0)

def compress_blocks(kv, pe, w1, w2):
    B, T, G, dh = kv.shape
    n_sub = T // CMP_STRIDE
    n_cmp = n_sub - CMP_RATIO + 1
    sub = kv.reshape(B, n_sub, CMP_STRIDE, G, dh)
    blocks = jnp.concatenate([sub[:, i:i + n_cmp] for i in range(CMP_RATIO)], axis=2)
    blocks = blocks + pe[None, None, :, None, :]
    flat = blocks.transpose(0, 1, 3, 2, 4).reshape(B, n_cmp, G, CMP_BLOCK * dh)
    return jax.nn.gelu(flat @ w1) @ w2

def nsa_attention(q, k_cmp, v_cmp, k_slc, v_slc, k_win, v_win, gates,
                  pe_ck, w1_ck, w2_ck, pe_cv, w1_cv, w2_cv):
    B, T, H, dh = q.shape
    G = k_cmp.shape[2]
    scale = dh ** -0.5
    kc = compress_blocks(k_cmp, pe_ck, w1_ck, w2_ck)
    vc = compress_blocks(v_cmp, pe_cv, w1_cv, w2_cv)
    n_cmp = kc.shape[1]
    n_slc = T // SLC_BLOCK
    n_sel = min(TOP_N, n_slc)
    cmp_start = jnp.arange(n_cmp) * CMP_STRIDE
    cmp_end = cmp_start + CMP_BLOCK - 1
    slc_start = jnp.arange(n_slc) * SLC_BLOCK
    overlap = ((cmp_start[:, None] < slc_start[None, :] + SLC_BLOCK)
               & (slc_start[None, :] < cmp_start[:, None] + CMP_BLOCK)).astype(jnp.float32)
    ks_blocks = k_slc.reshape(B, n_slc, SLC_BLOCK, G, dh).transpose(0, 3, 1, 2, 4)
    vs_blocks = v_slc.reshape(B, n_slc, SLC_BLOCK, G, dh).transpose(0, 3, 1, 2, 4)
    kw_pad = jnp.pad(k_win, ((0, 0), (WINDOW, 0), (0, 0), (0, 0)))
    vw_pad = jnp.pad(v_win, ((0, 0), (WINDOW, 0), (0, 0), (0, 0)))
    qg = q.reshape(B, T, G, GROUP, dh)
    b_idx = jnp.arange(B)[:, None, None, None]
    g_idx = jnp.arange(G)[None, :, None, None]
    blk = jnp.arange(n_slc)
    span = NSA_Q_BLOCK + WINDOW
    Q = NSA_Q_BLOCK

    def block(i):
        q0 = i * Q
        qb = lax.dynamic_slice_in_dim(qg, q0, Q, axis=1)
        gb = lax.dynamic_slice_in_dim(gates, q0, Q, axis=1).reshape(B, Q, G, GROUP, 3)
        t = q0 + jnp.arange(Q)
        s = jnp.einsum('bqgrd,bcgd->bgrqc', qb, kc, preferred_element_type=jnp.float32) * scale
        p_cmp = masked_softmax(s, cmp_end[None, :] <= t[:, None])
        o_cmp = jnp.einsum('bgrqc,bcgd->bqgrd', p_cmp, vc)
        imp = jnp.einsum('bgrqc,cn->bgqn', p_cmp, overlap)
        cur = t // SLC_BLOCK
        visible = blk[None, :] <= cur[:, None]
        forced = (blk[None, :] == 0) | (blk[None, :] == cur[:, None]) | (blk[None, :] == cur[:, None] - 1)
        imp = jnp.where(forced, FORCE_SCORE, jnp.where(visible, imp, -1.0))
        _, idx = lax.top_k(imp, n_sel)
        ks = ks_blocks[b_idx, g_idx, idx]
        vs = vs_blocks[b_idx, g_idx, idx].reshape(B, G, Q, n_sel * SLC_BLOCK, dh)
        s = jnp.einsum('bqgrd,bgqnld->bgrqnl', qb, ks, preferred_element_type=jnp.float32) * scale
        s = s.reshape(B, G, GROUP, Q, n_sel * SLC_BLOCK)
        key_pos = idx[..., None] * SLC_BLOCK + jnp.arange(SLC_BLOCK)
        mask_s = (key_pos <= t[None, None, :, None, None]).reshape(B, G, 1, Q, n_sel * SLC_BLOCK)
        p = masked_softmax(s, mask_s)
        o_slc = jnp.einsum('bgrqm,bgqmd->bqgrd', p, vs)
        kw = lax.dynamic_slice_in_dim(kw_pad, q0, span, axis=1)
        vw = lax.dynamic_slice_in_dim(vw_pad, q0, span, axis=1)
        s = jnp.einsum('bqgrd,bkgd->bgrqk', qb, kw, preferred_element_type=jnp.float32) * scale
        kpos = q0 - WINDOW + jnp.arange(span)
        mask_w = (kpos[None, :] >= 0) & (kpos[None, :] <= t[:, None]) & (t[:, None] - kpos[None, :] < WINDOW)
        p = masked_softmax(s, mask_w)
        o_win = jnp.einsum('bgrqk,bkgd->bqgrd', p, vw)
        o = gb[..., 0:1] * o_cmp + gb[..., 1:2] * o_slc + gb[..., 2:3] * o_win
        return o.reshape(B, Q, H * dh).astype(q.dtype)

    out = lax.map(block, jnp.arange(T // Q))
    return out.transpose(1, 0, 2, 3).reshape(B, T, H * dh)

def forgetting_attention(q, k, v, log_f):
    B, T, H, dh = q.shape
    scale = dh ** -0.5
    cf = lax.cumsum(log_f, axis=1).transpose(0, 2, 1)
    kpos = jnp.arange(T)

    def block(i):
        q0 = i * Q_BLOCK
        qb = lax.dynamic_slice_in_dim(q, q0, Q_BLOCK, axis=1)
        cq = lax.dynamic_slice_in_dim(cf, q0, Q_BLOCK, axis=2)
        t = q0 + jnp.arange(Q_BLOCK)
        s = jnp.einsum('bqhd,bkhd->bhqk', qb, k, preferred_element_type=jnp.float32) * scale
        s = s + (cq[..., :, None] - cf[..., None, :])
        p = masked_softmax(s, kpos[None, :] <= t[:, None])
        o = jnp.einsum('bhqk,bkhd->bqhd', p, v)
        return o.reshape(B, Q_BLOCK, H * dh).astype(q.dtype)

    out = lax.map(block, jnp.arange(T // Q_BLOCK))
    return out.transpose(1, 0, 2, 3).reshape(B, T, H * dh)

def hybrid_mixer(h, positions, w_in, b_forget, pe_ck, w1_ck, w2_ck, pe_cv, w1_cv, w2_cv,
                 w_up_nsa, w_up_fox, w_o):
    B, T, _ = h.shape
    split_points = [int(s) for s in np.cumsum(IN_SIZES)[:-1]]
    (q_n, k_c, v_c, k_s, v_s, k_w, v_w, gate_n, q_f, k_f, v_f, f_logit,
     gm_nsa, gm_fox) = jnp.split(h @ w_in, split_points, axis=-1)

    def heads(a, n):
        return a.reshape(B, T, n, HEAD_DIM)

    o_nsa = nsa_attention(
        partial_rope(heads(q_n, N_HEADS_NSA), positions),
        partial_rope(heads(k_c, N_KV_NSA), positions), heads(v_c, N_KV_NSA),
        partial_rope(heads(k_s, N_KV_NSA), positions), heads(v_s, N_KV_NSA),
        partial_rope(heads(k_w, N_KV_NSA), positions), heads(v_w, N_KV_NSA),
        jax.nn.sigmoid(gate_n.reshape(B, T, N_HEADS_NSA, 3)),
        pe_ck, w1_ck, w2_ck, pe_cv, w1_cv, w2_cv)
    log_f = jax.nn.log_sigmoid((f_logit + b_forget).astype(jnp.float32))
    o_fox = forgetting_attention(heads(q_f, N_HEADS_FOX), heads(k_f, N_HEADS_FOX),
                                 heads(v_f, N_HEADS_FOX), log_f)
    merged = jax.nn.sigmoid(gm_nsa) * (o_nsa @ w_up_nsa) + jax.nn.sigmoid(gm_fox) * (o_fox @ w_up_fox)
    return merged @ w_o

def setup_inputs(seed: int = 0) -> dict:
    key = jax.random.key(seed)
    ks = jax.random.split(key, 32)
    L, D = DEPTH, D_MODEL

    def w(k, shape, fan_in, mult=1.0):
        return jax.random.normal(k, shape, jnp.float32) * (mult * fan_in ** -0.5)

    def gain(k, shape):
        return 1.0 + 0.05 * jax.random.normal(k, shape, jnp.float32)

    return {
        'x': jax.random.normal(ks[0], (BATCH, SEQ, D), jnp.float32),
        'c': jax.random.normal(ks[1], (BATCH, D), jnp.float32),
        'positions': (jnp.arange(SEQ, dtype=jnp.int32)[None, :]
                      + jax.random.randint(ks[2], (BATCH, 1), 0, 1024, dtype=jnp.int32)),
        'w_ada': w(ks[3], (L, D, N_MOD * D), D, 0.5),
        'b_ada': 0.02 * jax.random.normal(ks[4], (L, N_MOD * D), jnp.float32),
        'g_ffn1': gain(ks[5], (L, D)),
        'w_gate1': w(ks[6], (L, D, D_FF), D),
        'w_up1': w(ks[7], (L, D, D_FF), D),
        'w_down1': w(ks[8], (L, D_FF, D), D_FF),
        'g_mix': gain(ks[9], (L, D)),
        'w_in': w(ks[10], (L, D, D_IN), D),
        'b_forget': 3.0 + 0.5 * jax.random.normal(ks[11], (L, N_HEADS_FOX), jnp.float32),
        'pe_ck': 0.5 * jax.random.normal(ks[12], (L, CMP_BLOCK, HEAD_DIM), jnp.float32),
        'w1_ck': w(ks[13], (L, CMP_BLOCK * HEAD_DIM, CMP_HIDDEN), CMP_BLOCK * HEAD_DIM),
        'w2_ck': w(ks[14], (L, CMP_HIDDEN, HEAD_DIM), CMP_HIDDEN),
        'pe_cv': 0.5 * jax.random.normal(ks[15], (L, CMP_BLOCK, HEAD_DIM), jnp.float32),
        'w1_cv': w(ks[16], (L, CMP_BLOCK * HEAD_DIM, CMP_HIDDEN), CMP_BLOCK * HEAD_DIM),
        'w2_cv': w(ks[17], (L, CMP_HIDDEN, HEAD_DIM), CMP_HIDDEN),
        'w_up_nsa': w(ks[18], (L, D_NSA, D), D_NSA),
        'w_up_fox': w(ks[19], (L, D_FOX, D), D_FOX),
        'w_o': w(ks[20], (L, D, D), D),
        'g_ffn2': gain(ks[21], (L, D)),
        'w_gate2': w(ks[22], (L, D, D_FF), D),
        'w_up2': w(ks[23], (L, D, D_FF), D),
        'w_down2': w(ks[24], (L, D_FF, D), D_FF),
        'g_final': gain(ks[25], (D,)),
    }

def reference(x, c, positions, w_ada, b_ada, g_ffn1, w_gate1, w_up1, w_down1, g_mix, w_in,
              b_forget, pe_ck, w1_ck, w2_ck, pe_cv, w1_cv, w2_cv, w_up_nsa, w_up_fox, w_o,
              g_ffn2, w_gate2, w_up2, w_down2, g_final):
    c_act = jax.nn.silu(c)
    for l in range(DEPTH):
        mod = c_act @ w_ada[l] + b_ada[l]
        sh1, sc1, ga1, sh2, sc2, ga2, sh3, sc3, ga3 = jnp.split(mod, N_MOD, axis=-1)
        h = modulate(rms_norm(x, g_ffn1[l]), sh1, sc1)
        x = x + 0.5 * ga1[:, None, :] * swiglu(h, w_gate1[l], w_up1[l], w_down1[l])
        h = modulate(rms_norm(x, g_mix[l]), sh2, sc2)
        y = hybrid_mixer(h, positions, w_in[l], b_forget[l], pe_ck[l], w1_ck[l], w2_ck[l],
                         pe_cv[l], w1_cv[l], w2_cv[l], w_up_nsa[l], w_up_fox[l], w_o[l])
        x = x + ga2[:, None, :] * y
        h = modulate(rms_norm(x, g_ffn2[l]), sh3, sc3)
        x = x + 0.5 * ga3[:, None, :] * swiglu(h, w_gate2[l], w_up2[l], w_down2[l])
    return rms_norm(x, g_final)


_drawn_inputs = setup_inputs


def setup_inputs(seed=0):
    import zlib

    import numpy as np

    out = dict(_drawn_inputs(seed))
    spreads = {}
    factors = {'b_ada': 3.886,
     'g_ffn1': 6.812,
     'g_mix': 8.0,
     'b_forget': 3.86,
     'pe_ck': 8.0,
     'w1_ck': 5.323,
     'w2_ck': 5.494,
     'g_ffn2': 7.317,
     'pe_cv': 6.234}
    for name, (base, spread) in spreads.items():
        noise = np.random.default_rng([zlib.crc32(name.encode()), seed]).standard_normal(out[name].shape)
        drawn = base * np.exp(spread * noise) if base else spread * noise
        out[name] = __import__('jax').numpy.asarray(drawn.astype(out[name].dtype))
    for name, factor in factors.items():
        out[name] = (out[name] * factor).astype(out[name].dtype)
    return out
```

```python
from contextlib import ExitStack

import concourse.bass as bass
from concourse import mybir

F32 = mybir.dt.float32
F32R = mybir.dt.float32r
BF16 = mybir.dt.bfloat16
I32 = mybir.dt.int32
ALU = mybir.AluOpType
ACT = mybir.ActivationFunctionType
AX = mybir.AxisListType

P = 128
D = 1024
T = 1024
NT = D // P
HALF = 512
NH = T // HALF
FF = 2816
NF = FF // P
EPS = 1e-6
N_MOD = 9
HD = 64
N_CMP = 63
SCALE = HD ** -0.5
SEQ_TILES = 43
LOG_COEFS = tuple(1.0 / k for k in range(17, 1, -2))
FL_STEPS = 3 + 4 + len(LOG_COEFS) + 3
TWO_PI_PARTS = (6.28125, 0.0019350051879882812, 3.0199157663446274e-07)
SWAP = [(k + 8) % 16 if k < 16 else k for k in range(32)]
ROUND = 12582912.0
SH1, SC1, GA1, SH2, SC2, GA2, SH3, SC3, GA3 = range(N_MOD)


def halves(h):
    return slice(h * HALF, (h + 1) * HALF)


class Plan:

    def __init__(self, units, group_units, before=None, times=0):
        self.units = units
        self.rows = 4 * len(units)
        self.blocks = [(u, j) for u, lens in enumerate(units) for j in range(max(lens))]
        self.first = [sum(max(l) for l in units[:u]) for u in range(len(units) + 1)]
        self.groups = len(units) // group_units
        self.group_units = group_units
        self.row0, self.block0, self.group0 = (times * before.rows, times * len(before.blocks), times * before.groups) if before else (0, 0, 0)
        self.steps = self.rows + 5
        self.at = [[] for _ in range(self.steps)]
        for u, lens in enumerate(units):
            n = max(lens)
            for k in range(4):
                self.at[4 * u + 5 + k] += range(self.first[u] + n * k // 4, self.first[u] + n * (k + 1) // 4)

    def length(self, s):
        return self.units[s // 4][s % 4]

    def first_row(self, b):
        u, j = self.blocks[b]
        return next(r for r in range(4) if self.units[u][r] > j)

    def group(self, b):
        return self.blocks[b][0] // self.group_units

    def starts(self, b):
        return b == self.first[self.group(b) * self.group_units]

    def last(self, og):
        return self.first[(og + 1) * self.group_units] - 1

    def due(self, b, behind):
        return [og for og in range(self.groups) if self.last(og) + behind == b]

    def left(self, behind):
        return [og for og in range(self.groups) if self.last(og) + behind >= len(self.blocks)]


WIN_TILES = 512 // P
CMP, SLC, WIN = range(3)
NSA_UNITS = [(i, br) for i in range(NT) for br in range(3)]
NSA = Plan([[(1, i + 1, min(i, WIN_TILES) + 1)[br]] * 4 for i, br in NSA_UNITS], 3)
FOX_UNITS = [(h, G) for h in range(2) for G in range(2)]
FOX = Plan([[4 * G + r + 1 for r in range(4)] for h, G in FOX_UNITS], 1, NSA, 2)
NEG = -1e30


def build(nc, aps, outs):
    ctx = ExitStack()
    with ctx:
        def sb(name, shape, dt=F32):
            return ctx.enter_context(nc.sbuf_tensor(name, shape, dt))

        def sem(name):
            return ctx.enter_context(nc.semaphore(name))

        KW = T
        r_arena = sb("r_arena", [P, (16 + 6 + 6) * KW], F32R)
        f_arena = sb("f_arena", [P, (8 + 3 + 10) * KW])

        def rt(at, n=1):
            return r_arena[:, at * KW:(at + n) * KW]

        def ft(at, n=1):
            return f_arena[:, at * KW:(at + n) * KW]

        h_hi = rt(0, 8).rearrange("p (n t) -> p n t", n=NT)
        h_lo = rt(8, 8).rearrange("p (n t) -> p n t", n=NT)
        w_hi = [rt(16 + 2 * b) for b in range(3)]
        w_lo = [rt(17 + 2 * b) for b in range(3)]
        x = ft(0, 8).rearrange("p (n t) -> p n t", n=NT)
        w_raw = [ft(8 + b) for b in range(3)]
        act_hi, act_lo = rt(22), rt(23)
        sq_hi = rt(24).rearrange("p (r t) -> p r t", r=2)
        sq_lo = rt(25).rearrange("p (r t) -> p r t", r=2)
        silu_g, act_f = ft(11), ft(12)
        ada_raw = ft(13, 4).rearrange("p (r t) -> p r t", r=4)
        ada_acc = ft(17)
        sq_f = ft(18).rearrange("p (r t) -> p r t", r=2)
        nrm_u = sq_f
        nrm_t = ft(20).rearrange("p (r t) -> p r t", r=2)
        rstd = ft(19)
        gains = sb("gains_sb", [P, 4, NT])
        b_ada = sb("b_ada_sb", [P, N_MOD, NT])
        mods = sb("mods", [P, N_MOD, NT])
        mods_half = sb("mods_half", [P, N_MOD, NT])
        c_raw = sb("c_raw", [P, NT])
        c_act = sb("c_act", [P, NT])
        nrm_a = sb("nrm_a", [P, 3, NT])
        nrm_s = sb("nrm_s", [P, 3, NT])
        ones_f = sb("ones_f", [P, P])
        ones_r = sb("ones_r", [P, P], F32R)
        eps = sb("eps", [P, 1])
        c_scratch = sb("c_scratch", [P, 1])
        c_scratch2 = sb("c_scratch2", [P, 1])

        ps = ctx.enter_context(nc.psum_tensor("ps", [P, 8, HALF], F32))
        ps_gate = ps[:, 0:2, :].rearrange("p a b -> p (a b)")
        ps_up = ps[:, 2:4, :].rearrange("p a b -> p (a b)")
        ps_down = [ps[:, 2 + k, :] for k in range(4)]
        ps_stat = ps[:, 6:8, :].rearrange("p a b -> p (a b)")

        rt_f = [ft(11), ft(12)]
        rope_s, rope_c, rope_w = ft(13), ft(14), ft(15)
        blk_f = ft(16, 2).rearrange("p (j g c) -> p j g c", j=16, g=2)
        pairs = [[ft(18), ft(19)], [ft(20), ft(10)]]
        q_hi, q_lo = [rt(22), rt(24)], [rt(23), rt(25)]
        blk_hi = rt(22, 2).rearrange("p (j m) -> p j m", j=16)
        blk_lo = rt(24, 2).rearrange("p (j m) -> p j m", j=16)
        v_st = rt(26, 2).rearrange("p (b h m) -> p b h m", b=NT, h=2)
        cf_hi, cf_lo, ncf_hi, ncf_lo = rt(20)[0:8], rt(21)[0:8], rt(20)[32:40], rt(21)[32:40]
        mix_ps = [ps_gate, ps_up]
        ps_v = ps[:, 4:6, :].rearrange("p a (b h d) -> p (a b) h d", h=2, d=HD)
        zero = sb("zero", [P, 1])
        ident_f = sb("ident_f", [P, P])
        gate_t = sb("gate_t", [P, NT, 24])
        rope_k = sb("rope_consts", [P, 2])
        pe2 = sb("pe2", [P, 2, 16])
        b_fg = sb("b_fg", [P, 1])
        w2_f = sb("w2_f", [P, 2, P])
        w2_hi = rt(26)[:, 0:2 * P].rearrange("p (k m) -> p k m", k=2)
        w2_lo = rt(26)[:, 2 * P:4 * P].rearrange("p (k m) -> p k m", k=2)
        hid_a = sb("hid_a", [P, P])
        hid_f = sb("hid_f", [P, P])
        hid_hi = rt(26)[:, 4 * P:5 * P]
        hid_lo = rt(26)[:, 5 * P:6 * P]
        kc_hi = sb("kc_hi", [P, P], F32R)
        kc_lo = sb("kc_lo", [P, P], F32R)
        vc_st = sb("vc_st", [P, P], F32R)
        lf = [sb(f"lf{i}", [P, HD]) for i in range(6)]

        q_n = [rt(r) for r in range(4)]
        k1_n, k2_n, v_n = [None, rt(4), rt(6)], [None, rt(5), rt(7)], [None, rt(8), rt(9)]
        q1_f, q2_f, k1_f, k2_f, v_f = ([rt(a), rt(b)] for a, b in ((22, 0), (23, 15), (24, 1), (25, 14), (26, 2)))
        pt = [rt(10 + k) for k in range(3)]
        o_st = rt(13)[0:HD]
        p_ring = [ft(11 + k) for k in range(8)]
        masks = ft(19, 2).bitcast(BF16)
        cmp_mask, causal, far_edge, ident_b = masks[:, 0:2048], masks[:, 2048:2176], masks[:, 2176:2304], masks[:, 2304:2432]
        o_sum = ft(20)[0:HD, HALF:T]
        negmax = sb("negmax", [P, 8])
        rowsum = sb("rowsum", [P, 8])
        rinv = sb("rinv", [P, 8])
        gate_g = sb("gate_g", [P, NT, 12])
        o_hi = [rt(k) for k in (3, 4, 5, 6, 0, 1, 2, 10)]
        o_lo = [rt(k) for k in (7, 8, 9, 27, 11, 12, 14, 15)]
        sg = [ft(13), ft(14)]
        part = [ft(15), ft(16)]
        ps_ring2 = [ps[:, 4 + k, :] for k in range(4)]

        def scratch(name, shape, dt=F32):
            return nc.dram_tensor(name, shape, dt, kind="Internal").ap()
        qk_d = [scratch("qk_hi_d", (14, P, T)), scratch("qk_lo_d", (14, P, T))]
        v_d = scratch("v_d", (6, P, 2 * T))
        cf_d = scratch("cf_d", (4, 8, T))
        sg_d = scratch("sg_d", (16, P, T))
        o_d = scratch("o_d", (2, 8, P, T))
        o_heads = [o_d[k].rearrange("n (e d) t -> (n e) d t", e=2) for k in range(2)]

        s_small = sem("small_in")
        s_x = [sem(f"x_in{n}") for n in range(NT)]
        s_ada = [sem(f"ada_in{r}") for r in range(4)]
        s_ada_used = sem("ada_used")
        s_mod_mm = sem("mod_mm")
        s_mods = sem("mods_done")
        s_c = sem("c_act")
        s_const = sem("const")
        s_raw = [[sem(f"raw{f}{b}") for b in range(3)] for f in range(3)]
        s_out = sem("out_done")

        nsem = {n: sem(f"n_{n}") for n in ("sq", "hi", "lo", "mm", "std", "rstd", "u", "t", "hh", "hl", "ab")}

        def ffn_sems(f):
            return {n: sem(f"f{f}_{n}") for n in ("hg", "hu", "hd", "lg", "lu", "ld", "gate", "up", "down", "x", "silu", "act", "ah", "al")}
        fsem = [ffn_sems(f) for f in range(2)]
        OUT = 2
        osem = {n: sem(f"o_{n}") for n in ("hu", "hd", "lu", "ld", "upa", "up", "down", "x", "pa", "pb", "act", "ah", "al", "sga", "sgb")}
        fsem.append(osem)
        asem = {n: sem(f"a_{n}") for n in ("sd", "mx", "ex", "ri", "sc", "tr", "ph", "pl", "pv", "oa", "oo", "oh", "ol", "st")}
        s_nq, s_nk, s_nv = sem("nsa_q_in"), [None, sem("nsa_ks_in"), sem("nsa_kw_in")], sem("nsa_v_in")
        s_fox = [sem("fox_in_a"), sem("fox_in_b")]
        s_gate, s_mask, s_fill = sem("gate_g"), sem("masks"), sem("fill")
        s_on, s_of = sem("o_nsa_in"), sem("o_fox_in")
        s_fin = sem("final")
        s_taken = sem("rows_taken")

        psem = {n: [sem(f"p_{n}{b}") for b in range(2)] for n in
                ("raw", "wh", "wl", "mm", "free", "rt", "qh", "ql", "st", "pair")}
        q_ = {n: sem(f"q_{n}") for n in
              ("const", "w", "rope", "pos", "sin", "own", "blk", "bh", "bl", "w2", "cmp",
               "gsg", "gtr", "gt", "frow", "fz", "fl", "cf", "cfd", "vtr", "vh", "vl", "vst", "fe")}

        def chain(step, kv):
            steps = ("ha", "hs", "gel", "tr", "hh", "hl", "cm2", "ch", "cl")
            return len(steps) * kv + steps.index(step) + 1


        def s_at(n):
            return P if n == 5 else 0

        def s_ps(s, n):
            bank = 2 * (s % 2)
            return ps[:, bank:bank + 2, :].rearrange("p a b -> p (a b)")[:, s_at(n):s_at(n) + n * P]

        block = ctx.enter_context(nc.Block())

        w_of = [(aps["wg1"], aps["wu1"], aps["wd1"]), (aps["wg2"], aps["wu2"], aps["wd2"]), (None, aps["w_up"], aps["w_o"])]
        G, U, DN = range(3)

        @block.sync
        def _(sp):
            sp.dma_start(c_raw[:], aps["c"]).then_inc(s_small, 16)
            sp.dma_start(b_ada[:], aps["b_ada"]).then_inc(s_small, 16)
            sp.dma_start(gains[:], aps["gains"]).then_inc(s_small, 16)
            for tile, name in ((rope_k, "rope_k"), (pe2, "pe2"), (b_fg, "b_fg"), (w2_f, "w2")):
                sp.dma_start(tile[:], aps[name]).then_inc(s_small, 16)
            for n in range(NT):
                sp.dma_start(x[:, n, :], aps["xT"][n]).then_inc(s_x[n], 16)

            def ada(q, j=None):
                j = q // NT if j is None else j
                sp.dma_start(ada_raw[:, q % 4, :],
                             aps["w_ada"][(q % NT) * P:(q % NT + 1) * P, bass.ds(j * D, D)]).then_inc(s_ada[q % 4], 16)

            def weight(f, b, k):
                sp.dma_start(w_raw[b], w_of[f][b][k]).then_inc(s_raw[f][b], 16)

            def ffn_loads(f, with_ada):
                s = fsem[f]
                for k in (1, 2):
                    sp.wait_ge(s["lg"], k)
                    weight(f, G, k)
                    sp.wait_ge(s["ld" if k == 2 else "lu"], 1)
                    if k == 1:
                        weight(f, U, 1)
                    else:
                        weight(f, DN, 1)
                        sp.wait_ge(s["lu"], 2)
                        weight(f, U, 2)

                def body(i, ada_too):
                    if ada_too:
                        for m in range(4):
                            sp.wait_ge(s_ada_used, 8 * i + 13 + m)
                            ada(m, i + 2)
                    sp.wait_ge(s["lg"], i + 2)
                    weight(f, G, i + 2)
                    sp.wait_ge(s["ld"], i + 1)
                    weight(f, DN, i + 1)
                    if ada_too:
                        for m in range(4, 8):
                            sp.wait_ge(s_ada_used, 8 * i + 13 + m)
                            ada(m, i + 2)
                    sp.wait_ge(s["lu"], i + 2)
                    weight(f, U, i + 2)

                if with_ada:
                    with sp.Fori(1, 7) as i:
                        body(i, True)
                with sp.Fori(7 if with_ada else 1, NF - 2) as i:
                    body(i, False)
                sp.wait_ge(s["ld"], NF - 1)
                weight(f, DN, NF - 1)

            for q in range(3 * NT):
                if q >= 4:
                    sp.wait_ge(s_ada_used, q - 3)
                ada(q)
                if q == 3:
                    weight(0, G, 0)
                if q == 15:
                    weight(0, U, 0)
            weight(0, DN, 0)
            ffn_loads(0, True)

            def mix_weight(b, i):
                sp.dma_start(w_raw[b], aps["wmix"][2 * i + b]).then_inc(psem["raw"][b], 16)
            sp.wait_ge(fsem[0]["lg"], NF)
            mix_weight(0, 0)
            sp.wait_ge(fsem[0]["lu"], NF)
            mix_weight(1, 0)
            with sp.Fori(1, 21) as i:
                for b in range(2):
                    sp.wait_ge(psem["wl"][b], i)
                    mix_weight(b, i)
            sp.wait_ge(psem["wl"][0], 21)
            mix_weight(0, 21)

            a = asem
            sp.wait_ge(q_["blk"], 9)
            weight(OUT, DN, 0)
            sp.wait_ge(psem["wl"][1], 21)
            weight(OUT, U, 0)
            sp.wait_ge(psem["mm"][1], 21)
            sp.wait_ge(psem["mm"][0], 22)
            for b in range(2):
                sp.wait_ge(psem["st"][b], 352)

            def nsa_queries_keys(g):
                for r in range(4):
                    for k in range(2):
                        sp.dma_start(q_n[r][k * HD:(k + 1) * HD].bitcast(F32),
                                     qk_d[k][2 + 2 * g + r // 2, (r % 2) * HD:(r % 2 + 1) * HD]).then_inc(s_nq, 16)
                for br in (SLC, WIN):
                    for k, tile in enumerate((k1_n[br], k2_n[br])):
                        for e in range(2):
                            sp.dma_start(tile[e * HD:(e + 1) * HD].bitcast(F32),
                                         qk_d[k][br - 1, g * HD:(g + 1) * HD]).then_inc(s_nk[br], 16)

            def nsa_values(g):
                for br in (SLC, WIN):
                    sp.dma_start(v_n[br].bitcast(F32).rearrange("p (b m) -> p b m", b=NT),
                                 v_d[br - 1].rearrange("p (b h m) -> p b h m", b=NT, h=2)[:, :, g]).then_inc(s_nv, 16)

            def nsa_store(g, i):
                sp.wait_ge(a["ol"], g * NT + i + 1)
                for k in range(2):
                    sp.dma_start(o_heads[k][4 * g:4 * g + 4, :, i * P:(i + 1) * P].rearrange("h d t -> d h t"),
                                 o_st[:, halves(k)].bitcast(F32).rearrange("d (h t) -> d h t", h=4)).then_inc(a["st"], 16)
            nsa_queries_keys(0)
            sp.wait_ge(q_["vst"], 96)
            sp.wait_ge(q_["cfd"], 64)
            nsa_values(0)

            def fox_load(e, p):
                rows = slice(e * HD, (e + 1) * HD)
                for tile, k, j in ((q1_f, 0, 6), (q2_f, 0, 6), (k2_f, 1, 7)):
                    sp.dma_start(tile[e][0:HD].bitcast(F32), qk_d[k][p * 2 + j, rows]).then_inc(s_fox[e], 16)
                sp.dma_start(q1_f[e][HD:P].bitcast(F32), qk_d[1][p * 2 + 6, rows]).then_inc(s_fox[e], 16)
                for k in range(2):
                    sp.dma_start(k1_f[e][k * HD:(k + 1) * HD].bitcast(F32), qk_d[0][p * 2 + 7, rows]).then_inc(s_fox[e], 16)
                for k in range(2):
                    sp.dma_start(q2_f[e][HD + k:HD + k + 1].bitcast(F32), cf_d[k, bass.ds(p * 2 + e, 1)]).then_inc(s_fox[e], 16)
                    sp.dma_start(k2_f[e][HD + 2 + k:HD + 3 + k].bitcast(F32),
                                 cf_d[2 + k, bass.ds(p * 2 + e, 1)]).then_inc(s_fox[e], 16)
                sp.dma_start(v_f[e].bitcast(F32).rearrange("p (b m) -> p b m", b=NT),
                             v_d[p + 2].rearrange("p (b h m) -> p b h m", b=NT, h=2)[:, :, e]).then_inc(s_fox[e], 16)
            sp.wait_ge(s_fill, 8)
            fox_load(0, 0)
            for i in range(NT - 1):
                nsa_store(0, i)
            sp.wait_ge(a["sd"], NSA.rows)
            nsa_queries_keys(1)
            sp.wait_ge(a["pv"], len(NSA.blocks))
            nsa_values(1)
            for i in range(NT - 1, 2 * NT):
                nsa_store(i // NT, i % NT)
            sp.wait_ge(a["pv"], 2 * len(NSA.blocks))
            fox_load(1, 0)
            sp.wait_ge(a["st"], 32 * (2 * NT + 1))
            for n in range(4):
                for k, tile in enumerate((o_hi[n], o_lo[n])):
                    sp.dma_start(tile.bitcast(F32), o_d[k][n]).then_inc(s_on, 16)

            def fox_store(p, e, half):
                sp.wait_ge(a["ol"], p * 4 + (FOX.group0 + 2 * e + half + 1))
                for k in range(2):
                    sp.dma_start(o_heads[k][bass.ds(p * 2 + (8 + e), 1), :, halves(half)].rearrange("h d t -> d (h t)"),
                                 o_st[:, halves(k)].bitcast(F32)).then_inc(a["st"], 16)

            with sp.Fori(0, 3) as p:
                fox_store(p, 0, 0)
                sp.wait_ge(a["pv"], p * len(FOX.blocks) + (FOX.block0 + FOX.first[2]))
                fox_load(0, p + 1)
                fox_store(p, 0, 1)
                fox_store(p, 1, 0)
                sp.wait_ge(a["pv"], p * len(FOX.blocks) + (FOX.block0 + len(FOX.blocks)))
                fox_load(1, p + 1)
                fox_store(p, 1, 1)
            for e in range(2):
                for half in range(2):
                    fox_store(3, e, half)
            sp.wait_ge(a["st"], 32 * (4 * NT + 1))
            for n in range(4, NT):
                for k, tile in enumerate((o_hi[n], o_lo[n])):
                    sp.dma_start(tile.bitcast(F32), o_d[k][n]).then_inc(s_of, 16)

            s = osem

            def sg_load(e, m):
                sp.dma_start(sg[e], sg_d[m * 2 + e]).then_inc(s[("sga", "sgb")[e]], 16)
            sg_load(0, 0)
            sg_load(1, 0)
            sp.wait_ge(psem["wl"][0], 22)
            weight(1, G, 0)
            with sp.Fori(1, NT) as m:
                sp.wait_ge(s["lu"], m)
                weight(OUT, U, m)
                sp.wait_ge(s["ld"], m)
                weight(OUT, DN, m)
                sp.wait_ge(s["pa"], m)
                sg_load(0, m)
                sp.wait_ge(s["pb"], m)
                sg_load(1, m)
            sp.wait_ge(s["lu"], NT)
            weight(1, U, 0)
            sp.wait_ge(s["ld"], NT)
            weight(1, DN, 0)
            ffn_loads(1, False)
            for j in range(16):
                sp.wait_ge(s_fin, j + 1)
                sp.dma_start(outs["outT"][j // 2, :, halves(j % 2)], x[:, j // 2, halves(j % 2)]).then_inc(s_out, 16)
            sp.wait_ge(s_out, 256)

        @block.scalar
        def _(act):
            act.wait_ge(s_small, 112)
            act.activation(c_act[:], c_raw[:], ACT.Silu).then_inc(s_c, 1)

            def square(k, j, ready):
                s = nsem
                ready(act, j)
                if j >= 2:
                    act.wait_ge(s["lo"], 16 * k + j - 1)
                act.activation(sq_f[:, j % 2, :], x[:, j // 2, halves(j % 2)], ACT.Square).then_inc(s["sq"], 1)

            def std(k):
                s = nsem
                for h in range(NH):
                    act.wait_ge(s["mm"], 16 * k + 15 + h)
                    act.activation(rstd[:, halves(h)], ps_stat[:, halves(h)], ACT.Sqrt, bias=eps[:, 0:1],
                                   scale=1.0 / D).then_inc(s["std"], 1)

            def apply(k):
                s = nsem
                for m in range(NT * NH):
                    act.wait_ge(s["t"], 16 * k + m + 1)
                    act.copy(h_hi[:, m % NT, halves(m // NT)], nrm_t[:, m % 2, :]).then_inc(s["hh"], 1)

            def x_loaded(e, j):
                e.wait_ge(s_x[j // 2], 16)

            def ffn_hi(f, b, k):
                act.wait_ge(s_raw[f][b], 16 * (k + 1))
                act.copy(w_hi[b], w_raw[b]).then_inc(fsem[f][("hg", "hu", "hd")[b]], 1)

            def silu(f, i, first=False):
                s = fsem[f]
                act.wait_ge(s["gate"], i + 1)
                if not first:
                    act.wait_ge(s["act"], i)
                act.activation(silu_g, ps_gate, ACT.Silu).then_inc(s["silu"], 1)

            def act_high(f, i):
                s = fsem[f]
                act.wait_ge(s["act"], i + 1)
                act.copy(act_hi, act_f).then_inc(s["ah"], 1)

            def ffn(f):
                s = fsem[f]
                silu(f, 0, True)
                ffn_hi(f, G, 1)
                if f == 1:
                    act.wait_ge(osem["down"], NT * 16)
                ffn_hi(f, DN, 0)
                act.wait_ge(s["up"], 1)
                ffn_hi(f, U, 1)
                act_high(f, 0)
                def body(i):
                    silu(f, i)
                    ffn_hi(f, G, i + 1)
                    act.wait_ge(s["down"], i * 16)
                    ffn_hi(f, DN, i)
                    act.wait_ge(s["up"], i + 1)
                    ffn_hi(f, U, i + 1)
                    act_high(f, i)
                if f == 0:
                    with act.Fori(1, 11) as i:
                        body(i)
                    for k, table in enumerate((rope_s, rope_c)):
                        act.wait_ge(q_["rope"], k + 1)
                        act.activation(table, table, ACT.Sin).then_inc(q_["sin"], 1)
                with act.Fori(11 if f == 0 else 1, NF - 1) as i:
                    body(i)
                i = NF - 1
                silu(f, i)
                act.wait_ge(s["down"], i * 16)
                ffn_hi(f, DN, i)
                act_high(f, i)

            def x_added(base, s):
                return lambda e, j: e.wait_ge(s, base + j + 1)

            def w_high(b, k):
                act.wait_ge(psem["raw"][b], 16 * (k + 1))
                act.copy(w_hi[b], w_raw[b]).then_inc(psem["wh"][b], 1)

            def pair_up(kv, b):
                for g in range(2):
                    rows = rt_f[b][g * HD:(g + 1) * HD]
                    act.dma_start(pairs[kv][g][0:HD, :], rows).then_inc(psem["pair"][kv], 16)
                    act.dma_start(pairs[kv][g][HD:P, 0:T - 1], rows[:, 1:T]).then_inc(psem["pair"][kv], 16)

            def gm(b, m, use, first=False):
                act.wait_ge(psem["mm"][b], use + 1)
                if not first:
                    act.wait_ge(psem["st"][b], m * 16)
                act.activation(rt_f[b], mix_ps[b], ACT.Sigmoid).then_inc(psem["rt"][b], 1)
                w_high(b, use + 1)
                act.wait_ge(psem["rt"][b], m + 2)
                act.dma_start(sg_d[m * 2 + 1 - b], rt_f[b]).then_inc(psem["st"][b], 16)

            def blocks_high(kv):
                act.wait_ge(q_["blk"], 4 * kv + 5)
                if kv == 1:
                    act.wait_ge(psem["mm"][0], 3)
                act.copy(rt(22, 2), ft(16, 2)).then_inc(q_["bh"], 1)

            def hidden(kv):
                act.wait_ge(psem["mm"][0], (3, 12)[kv])
                act.copy(hid_a[:], ps[:, 4, P:2 * P]).then_inc(q_["cmp"], 1)
                act.wait_ge(q_["cmp"], chain("hs", kv))
                act.activation(hid_f[:], hid_f[:], ACT.Gelu_apprx_tanh).then_inc(q_["cmp"], 1)

            def hidden_t(kv):
                act.wait_ge(q_["cmp"], chain("tr", kv))
                act.copy(hid_hi[:], ps[:, 5, 0:P]).then_inc(q_["cmp"], 1)

            def compressed(kv):
                act.wait_ge(q_["cmp"], chain("cm2", kv))
                if kv == 0:
                    act.copy(kc_hi[:], ps[:, 4, 0:P]).then_inc(q_["cmp"], 1)
                else:
                    act.copy(vc_st[:, 0:HD], ps[:, 4, 0:HD]).then_inc(q_["cmp"], 1)

            def qk_store(b, n, j):
                act.wait_ge(psem["ql"][b], n + 1)
                act.dma_start(qk_d[0][j], q_hi[b].bitcast(F32)).then_inc(psem["st"][b], 16)
                act.dma_start(qk_d[1][j], q_lo[b].bitcast(F32)).then_inc(psem["st"][b], 16)

            def rope(b, m, use, factor):
                act.wait_ge(psem["rt"][b], m + 10)
                act.wait_ge(psem["st"][b], m * 32 + 128)
                act.activation(q_hi[b], rt_f[b], ACT.Copy, scale=factor).then_inc(psem["qh"][b], 1)
                w_high(b, use + 1)
                qk_store(b, m, m * 2 + 1 - b)

            def plain(b, m, use, factor):
                act.wait_ge(psem["mm"][b], use + 1)
                act.wait_ge(psem["st"][b], m * 32 + 224)
                act.activation(q_hi[b], mix_ps[b], ACT.Copy, scale=factor).then_inc(psem["qh"][b], 1)
                w_high(b, use + 1)
                qk_store(b, m + 3, m * 2 + 7 - b)

            def v_copy(b, m, use, more):
                act.wait_ge(psem["mm"][b], use + 1)
                act.copy(rt_f[b], mix_ps[b]).then_inc(psem["rt"][b], 1)
                if more:
                    w_high(b, use + 1)

            def v_high(n):
                act.wait_ge(q_["vtr"], n + 1)
                if n >= 1:
                    act.wait_ge(q_["vst"], 16 * n)
                act.copy(v_st[:, :, :, 0:HD], ps_v).then_inc(q_["vh"], 1)
                act.wait_ge(q_["vl"], n + 1)
                act.dma_start(v_d[n], rt(26, 2).bitcast(F32)).then_inc(q_["vst"], 16)

            def attend(plan, a, it):
                n_rows, n_blocks, n_groups = plan.rows, len(plan.blocks), plan.groups

                def exp(s):
                    u, length = s // 4, plan.length(s)
                    act.wait_ge(a["mx"], it * n_rows + (plan.row0 + s + 1))
                    if u >= 2 and s % 4 == 0:
                        act.wait_ge(a["tr"], it * n_blocks + (plan.block0 + plan.first[u - 1]))
                    act.activation(p_ring[s % 8][:, 0:length * P], s_ps(s, length), ACT.Exp, bias=negmax[:, s % 8:s % 8 + 1],
                                   accum_out=rowsum[:, s % 8:s % 8 + 1]).then_inc(a["ex"], 1)

                def high(b):
                    c = plan.first_row(b) * P
                    act.wait_ge(a["tr"], it * n_blocks + (plan.block0 + b + 1))
                    if b >= 3:
                        act.wait_ge(a["pv"], it * n_blocks + (plan.block0 + b - 2))
                    act.copy(pt[b % 3][:, c:HALF], ps[:, 4 + b % 2, c:HALF]).then_inc(a["ph"], 1)

                def o_upper(og):
                    act.wait_ge(a["pv"], it * n_blocks + (plan.block0 + plan.last(og) + 1))
                    if og >= 1:
                        act.wait_ge(a["ol"], it * n_groups + (plan.group0 + og))
                    act.copy(o_sum, ps[HD:P, 6 + og % 2, :]).then_inc(a["oa"], 1)

                def o_high(og):
                    act.wait_ge(a["oo"], it * n_groups + (plan.group0 + og + 3))
                    act.wait_ge(a["st"], it * (32 * n_groups) + 32 * (plan.group0 + og + 1))
                    act.copy(o_st[:, 0:HALF], o_sum).then_inc(a["oh"], 1)

                for s in range(plan.steps):
                    if 1 <= s <= n_rows:
                        exp(s - 1)
                    for b in plan.at[s]:
                        high(b)
                        for og in plan.due(b, 3):
                            o_upper(og)
                        for og in plan.due(b, 5):
                            o_high(og)
                left = [(plan.last(og) + 3, o_upper, og) for og in plan.left(3)] + [(plan.last(og) + 5, o_high, og) for og in plan.left(5)]
                for _, step, og in sorted(left, key=lambda e: e[0]):
                    step(og)

            act.wait_ge(s_const, 3)
            for j in range(16):
                square(0, j, x_loaded)
            std(0)
            ffn_hi(0, G, 0)
            ffn_hi(0, U, 0)
            apply(0)
            ffn(0)
            for j in range(16):
                square(1, j, x_added(4 + 16 * (NF - 1), fsem[0]["x"]))
            std(1)
            w_high(0, 0)
            w_high(1, 0)
            apply(1)
            act.copy(w2_hi[:], w2_f[:]).then_inc(q_["w2"], 1)
            act.wait_ge(psem["mm"][0], 1)
            w_high(0, 1)
            act.wait_ge(psem["rt"][0], 1)
            pair_up(0, 0)
            act.wait_ge(psem["mm"][1], 1)
            act.copy(rt_f[1], mix_ps[1]).then_inc(psem["rt"][1], 1)
            w_high(1, 1)
            act.wait_ge(psem["rt"][1], 1)
            pair_up(1, 1)
            blocks_high(0)
            act.wait_ge(psem["mm"][0], 2)
            act.wait_ge(psem["pair"][0], 64)
            act.activation(rt_f[0], mix_ps[0], ACT.Sigmoid).then_inc(q_["gsg"], 1)
            w_high(0, 2)
            act.wait_ge(q_["gsg"], 1)
            act.copy(rt_f[0][0:8, :], mix_ps[0][0:8, :]).then_inc(psem["free"][0], 1)
            act.wait_ge(psem["free"][0], 2)
            act.dma_start(lf[0][:], rt_f[0][0:8, :]).then_inc(q_["fz"], 16)
            act.wait_ge(psem["mm"][1], 2)
            w_high(1, 2)
            act.wait_ge(psem["mm"][0], 3)
            w_high(0, 3)
            hidden(0)
            act.wait_ge(q_["fl"], 3)
            act.activation(lf[2][:], lf[1][:], ACT.Exp).then_inc(q_["fe"], 1)
            act.wait_ge(psem["pair"][1], 64)
            gm(1, 0, 2, first=True)
            hidden_t(0)
            act.wait_ge(q_["gtr"], 1)
            act.wait_ge(q_["fz"], 16)
            gm(0, 0, 3, first=True)
            compressed(0)
            with act.Fori(1, 8) as m:
                gm(1, m, m + 2)
                gm(0, m, m + 3)
            blocks_high(1)
            act.wait_ge(q_["bl"], 2)
            act.wait_ge(q_["fl"], FL_STEPS)
            act.dma_start(ft(16)[0:8, :], lf[3][:]).then_inc(q_["frow"], 16)
            act.wait_ge(psem["mm"][1], 11)
            w_high(1, 11)
            act.wait_ge(psem["mm"][0], 12)
            w_high(0, 12)
            hidden(1)
            act.wait_ge(q_["cf"], 5)
            for k, rows in enumerate((cf_hi, cf_lo, ncf_hi, ncf_lo)):
                act.dma_start(cf_d[k], rows.bitcast(F32)).then_inc(q_["cfd"], 16)
            rope(1, 0, 11, 1.0)
            hidden_t(1)
            rope(0, 0, 12, 1.0)
            compressed(1)
            with act.Fori(1, 3) as m:
                rope(1, m, m + 11, SCALE)
                rope(0, m, m + 12, SCALE)
            with act.Fori(0, 4) as m:
                plain(1, m, m + 14, SCALE)
                plain(0, m, m + 15, 1.0)
            for n in range(6):
                v_copy(1 - n % 2, n // 2, n // 2 + (18, 19)[n % 2], n < 4)
                if n >= 1:
                    v_high(n - 1)
            v_high(5)
            act.wait_ge(psem["mm"][0], 22)
            ffn_hi(OUT, DN, 0)
            ffn_hi(OUT, U, 0)
            with act.Fori(0, 2) as g:
                attend(NSA, asem, g)
            with act.Fori(0, 4) as p:
                attend(FOX, asem, p)
            s = osem
            act.wait_ge(s["upa"], 1)
            act.wait_ge(s["up"], 1)
            ffn_hi(OUT, U, 1)
            act_high(OUT, 0)
            with act.Fori(1, NT - 1) as m:
                act.wait_ge(s["down"], m * 16)
                ffn_hi(OUT, DN, m)
                act.wait_ge(s["up"], m + 1)
                ffn_hi(OUT, U, m + 1)
                act_high(OUT, m)
            act.wait_ge(s["down"], (NT - 1) * 16)
            ffn_hi(OUT, DN, NT - 1)
            act_high(OUT, NT - 1)
            ffn_hi(1, G, 0)
            act.wait_ge(s["up"], NT)
            ffn_hi(1, U, 0)
            for j in range(16):
                square(2, j, x_added(4 + 16 * (NT - 1), s["x"]))
            std(2)
            apply(2)
            ffn(1)
            for j in range(16):
                square(3, j, x_added(4 + 16 * (NF - 1), fsem[1]["x"]))
            std(3)

        @block.gpsimd
        def _(pool):
            pool.memset(ones_f[:], 1.0).then_inc(s_const, 1)
            pool.memset(eps[:], EPS).then_inc(s_const, 1)
            pool.wait_ge(s_const, 2)
            pool.tensor_copy(ones_r[:], ones_f[:]).then_inc(s_const, 1)
            pool.memset(zero[:], 0.0).then_inc(q_["const"], 1)
            pool.memset(ident_f[:], 0.0).then_inc(q_["const"], 1)
            pool.wait_ge(q_["const"], 2)
            pool.affine_select(out=ident_f[:], in_=ident_f[:], compare_op=ALU.not_equal, fill=1.0, base=0,
                               pattern=[[-1, P]], channel_multiplier=1).then_inc(q_["const"], 1)

            def square_hi(k, j):
                s = nsem
                pool.wait_ge(s["sq"], 16 * k + j + 1)
                if j >= 2:
                    pool.wait_ge(s["mm"], 16 * k + j - 1)
                pool.tensor_scalar(sq_hi[:, j % 2, :], sq_f[:, j % 2, :], 1.0, 1.0, ALU.mult, ALU.mult).then_inc(s["hi"], 1)

            def apply(k):
                s = nsem
                pool.wait_ge(s["ab"], k + 1)
                for m in range(NT * NH):
                    n = m % NT
                    pool.wait_ge(s["u"], 16 * k + m + 1)
                    if m >= 2:
                        pool.wait_ge(s["hl"], 16 * k + m - 1)
                    pool.tensor_scalar(nrm_t[:, m % 2, :], nrm_u[:, m % 2, :], nrm_a[:, k, n:n + 1], nrm_s[:, k, n:n + 1],
                                       ALU.mult, ALU.add).then_inc(s["t"], 1)

            def ffn_lo(f, b, k):
                s = fsem[f]
                pool.wait_ge(s[("hg", "hu", "hd")[b]], k + 1)
                pool.tensor_tensor(w_lo[b], w_raw[b], w_hi[b].bitcast(F32), ALU.subtract).then_inc(s[("lg", "lu", "ld")[b]], 1)

            def rope_tables():
                steps = [0]

                def own(ins):
                    steps[0] += 1
                    ins.then_inc(q_["own"], 1)
                    pool.wait_ge(q_["own"], steps[0])
                ang, turns, part = ft(15), ft(16), ft(17)
                pool.wait_ge(s_mod_mm, N_MOD)
                pool.wait_ge(s_ada_used, N_MOD * NT)
                pool.dma_start(part.bitcast(I32), aps["pos"].partition_broadcast(P)).then_inc(q_["pos"], 16)
                pool.wait_ge(q_["pos"], 16)
                own(pool.tensor_copy(ang, part.bitcast(I32)))
                own(pool.tensor_scalar(ang, ang, rope_k[:, 0:1], 1.0, ALU.mult, ALU.mult))
                for r, ahead in ((rope_s, 0.0), (rope_c, 0.25)):
                    own(pool.tensor_scalar(turns, ang, 0.15915494309189535, ahead, ALU.mult, ALU.add))
                    own(pool.tensor_scalar(turns, turns, 1.0, ROUND, ALU.mult, ALU.add))
                    own(pool.tensor_scalar(turns, turns, 1.0, -ROUND, ALU.mult, ALU.add))
                    for k, c in enumerate(TWO_PI_PARTS):
                        own(pool.tensor_scalar(part, turns, -c, 1.0, ALU.mult, ALU.mult))
                        own(pool.tensor_tensor(r, ang if k == 0 else r, part, ALU.add))
                    if ahead:
                        own(pool.tensor_scalar(r, r, 1.0, 1.5707963267948966, ALU.mult, ALU.add))
                    pool.tensor_scalar(r, r, 3.1415925, -3.1415925, ALU.min, ALU.max).then_inc(q_["rope"], 1)

            def ffn(f):
                ffn_lo(f, G, 1)
                ffn_lo(f, DN, 0)
                ffn_lo(f, U, 1)

                def body(i):
                    ffn_lo(f, G, i + 1)
                    ffn_lo(f, DN, i)
                    ffn_lo(f, U, i + 1)
                if f == 0:
                    with pool.Fori(1, 8) as i:
                        body(i)
                    rope_tables()
                with pool.Fori(8 if f == 0 else 1, NF - 1) as i:
                    body(i)
                ffn_lo(f, DN, NF - 1)
                if f == 0:
                    pool.wait_ge(q_["sin"], 2)
                    pool.tensor_scalar(rope_s, rope_s, rope_k[:, 1:2], 1.0, ALU.mult, ALU.mult).then_inc(q_["rope"], 1)

            for j in range(16):
                square_hi(0, j)
            ffn_lo(0, G, 0)
            ffn_lo(0, U, 0)
            apply(0)
            ffn(0)
            for j in range(16):
                square_hi(1, j)

            def w_low(b, k):
                pool.wait_ge(psem["wh"][b], k + 1)
                pool.tensor_tensor(w_lo[b], w_raw[b], w_hi[b].bitcast(F32), ALU.subtract).then_inc(psem["wl"][b], 1)
            w_low(0, 0)
            w_low(1, 0)
            apply(1)
            with pool.Fori(1, 21) as k:
                w_low(0, k)
                w_low(1, k)
            w_low(0, 21)
            ffn_lo(OUT, DN, 0)
            ffn_lo(OUT, U, 0)

            def own(n, ins):
                ins.then_inc(s_mask, 1)
                pool.wait_ge(s_mask, n)
            pool.wait_ge(q_["blk"], 9)
            pool.wait_ge(q_["bl"], 2)
            own(1, pool.memset(cmp_mask, NEG))
            own(2, pool.memset(masks[:, 2048:2304], 0.0))
            for g in range(2):
                m = cmp_mask.rearrange("p (g i e c) -> p g i e c", g=2, i=NT, e=2)[:, g, :, g, :]
                own(3 + 2 * g, pool.memset(m, 0.0))
                own(4 + 2 * g, pool.affine_select(out=m, in_=m, compare_op=ALU.is_ge, fill=NEG, base=-31,
                                                  pattern=[[P, NT], [-16, HD]], channel_multiplier=1))
            own(7, pool.affine_select(out=causal, in_=causal, compare_op=ALU.is_ge, fill=NEG, base=0,
                                      pattern=[[-1, P]], channel_multiplier=1))
            own(8, pool.affine_select(out=far_edge, in_=far_edge, compare_op=ALU.is_ge, fill=NEG, base=-1,
                                      pattern=[[1, P]], channel_multiplier=-1))
            own(9, pool.tensor_copy(ident_b, ident_f[:]))
            pool.wait_ge(q_["gt"], 1)
            own(10, pool.affine_select(out=gate_t[:, 0, 0:24:3], in_=gate_t[:, 0, 0:24:3], compare_op=ALU.is_ge, fill=0.0, base=-31,
                                       pattern=[[0, 8]], channel_multiplier=1))
            pool.wait_ge(psem["mm"][0], 22)
            pool.wait_ge(psem["mm"][1], 21)
            for b in range(2):
                pool.wait_ge(psem["st"][b], 352)
            n = 0
            for tile in (q2_f[0], k2_f[0], q2_f[1], k2_f[1]):
                pool.memset(tile[HD:P].bitcast(F32), 0.0).then_inc(s_fill, 1)
                n += 2
                pool.wait_ge(s_fill, n - 1)
                pool.memset(tile[HD:HD + 4].bitcast(F32), 1.0).then_inc(s_fill, 1)

            pool.wait_ge(s_fill, 8)

            def attend(plan, a, it, gates=None):
                for s in range(plan.rows):
                    p = p_ring[s % 8][:, 0:plan.length(s) * P]
                    pool.wait_ge(a["ri"], it * plan.rows + (plan.row0 + s + 1))
                    pool.sem_inc(s_taken, 1)
                    pool.tensor_scalar(p, p, rinv[:, s % 8:s % 8 + 1], 1.0 if gates is None else gates(s), ALU.mult,
                                       ALU.mult).then_inc(a["sc"], 1)

            def nsa_gates(s):
                i, br = NSA_UNITS[s // 4]
                c = (s % 4) * 3 + br
                return gate_g[:, i, c:c + 1]
            with pool.Fori(0, 2) as g:
                pool.wait_ge(s_gate, g + 1)
                attend(NSA, asem, g, nsa_gates)
            with pool.Fori(0, 4) as p:
                attend(FOX, asem, p)

            def merge(m):
                s = osem
                pool.wait_ge(s["pa"], m + 1)
                pool.wait_ge(s["pb"], m + 1)
                pool.tensor_tensor(act_f, part[0], part[1], ALU.add).then_inc(s["act"], 1)
                pool.wait_ge(s["ah"], m + 1)
                pool.tensor_tensor(act_lo, act_f, act_hi.bitcast(F32), ALU.subtract).then_inc(s["al"], 1)
            ffn_lo(OUT, U, 1)
            merge(0)
            with pool.Fori(1, NT - 1) as m:
                ffn_lo(OUT, DN, m)
                ffn_lo(OUT, U, m + 1)
                merge(m)
            ffn_lo(OUT, DN, NT - 1)
            merge(NT - 1)
            ffn_lo(1, G, 0)
            ffn_lo(1, U, 0)
            for j in range(16):
                square_hi(2, j)
            apply(2)
            ffn(1)
            for j in range(16):
                square_hi(3, j)

        @block.vector
        def _(dve):
            def square_lo(k, j):
                s = nsem
                dve.wait_ge(s["hi"], 16 * k + j + 1)
                dve.tensor_tensor(sq_lo[:, j % 2, :], sq_f[:, j % 2, :], sq_hi[:, j % 2, :].bitcast(F32),
                                  ALU.subtract).then_inc(s["lo"], 1)

            def reciprocal(k, h):
                s = nsem
                dve.wait_ge(s["std"], 2 * k + h + 1)
                dve.reciprocal(rstd[:, halves(h)], rstd[:, halves(h)]).then_inc(s["rstd"], 1)

            def shift_scale(k):
                s = nsem
                sh, sc = 3 * k + SH1, 3 * k + SC1
                dve.wait_ge(s_mods, 2 * (sc + 1))
                dve.tensor_copy(nrm_s[:, k, :], mods[:, sh, :]).then_inc(s_const, 1)
                dve.wait_ge(s_const, 4 + k)
                dve.scalar_tensor_tensor(nrm_a[:, k, :], mods[:, sc, :], 1.0, gains[:, k, :], ALU.add,
                                         ALU.mult).then_inc(s["ab"], 1)

            def apply(k):
                s = nsem

                def scaled(m):
                    dve.wait_ge(s["rstd"], 2 * k + m // NT + 1)
                    if m >= 2:
                        dve.wait_ge(s["t"], 16 * k + m - 1)
                    dve.tensor_tensor(nrm_u[:, m % 2, :], x[:, m % NT, halves(m // NT)], rstd[:, halves(m // NT)],
                                      ALU.mult).then_inc(s["u"], 1)
                scaled(0)
                for m in range(NT * NH):
                    if m + 1 < NT * NH:
                        scaled(m + 1)
                    dve.wait_ge(s["hh"], 16 * k + m + 1)
                    h = (slice(None), m % NT, halves(m // NT))
                    dve.tensor_tensor(h_lo[h], nrm_t[:, m % 2, :], h_hi[h].bitcast(F32), ALU.subtract).then_inc(s["hl"], 1)

            def ada(q, m, used, first_wait=None):
                dve.wait_ge(s_ada[m % 4], used)
                w = ada_raw[:, m % 4, :]
                if m == 0:
                    if first_wait is not None:
                        dve.wait_ge(s_mod_mm, first_wait)
                    dve.tensor_scalar(ada_acc, w, c_act[:, 0:1], None, ALU.mult).then_inc(s_ada_used, 1)
                else:
                    dve.wait_ge(s_ada_used, q)
                    dve.scalar_tensor_tensor(ada_acc, w, c_act[:, m:m + 1], ada_acc, ALU.mult, ALU.add).then_inc(s_ada_used, 1)

            def mod(j, n):
                dve.wait_ge(s_mod_mm, n + 1)
                dve.tensor_tensor(mods[:, j, :], ps_stat[:, 0:NT], b_ada[:, j, :], ALU.add).then_inc(s_mods, 1)
                dve.wait_ge(s_mods, 2 * n + 1)
                dve.tensor_scalar(mods_half[:, j, :], mods[:, j, :], 0.5, None, ALU.mult).then_inc(s_mods, 1)

            def add_down(f, i, gate, ring=ps_down):
                s = fsem[f]
                dve.wait_ge(s["x"], 16 * (i - 1) + 4)
                for k in range(16):
                    n = k // 2
                    dve.wait_ge(s["down"], 16 * (i - 1) + k + 1)
                    xs = x[:, n, halves(k % 2)]
                    dve.scalar_tensor_tensor(xs, ring[k % 4], gate[:, n:n + 1], xs, ALU.mult, ALU.add).then_inc(s["x"], 1)

            def product(f, i, first=False):
                s = fsem[f]
                dve.wait_ge(s["up"], i + 1)
                dve.wait_ge(s["silu"], i + 1)
                if not first:
                    dve.wait_ge(s["al"], i)
                dve.tensor_tensor(act_f, silu_g, ps_up, ALU.mult).then_inc(s["act"], 1)
                dve.wait_ge(s["ah"], i + 1)
                dve.tensor_tensor(act_lo, act_f, act_hi.bitcast(F32), ALU.subtract).then_inc(s["al"], 1)

            dve.memset(c_scratch[:], 0.0).then_inc(fsem[0]["x"], 4)
            dve.memset(c_scratch2[:], 0.0).then_inc(fsem[1]["x"], 4)
            for n, c in ((osem["x"], 4), (asem["oo"], 2), (asem["st"], 32)):
                dve.memset(sb(f"credit{n.name}", [P, 1])[:], 0.0).then_inc(n, c)
            for j in range(16):
                square_lo(0, j)
            dve.wait_ge(s_c, 1)
            for q in range(8):
                ada(q, q, 16 * (q // 4 + 1))
            reciprocal(0, 0)
            reciprocal(0, 1)
            mod(SH1, 0)
            for q in range(8, 16):
                ada(q, q % 8, 16 * (q // 4 + 1), 1)
            mod(SC1, 1)
            shift_scale(0)
            apply(0)
            for q in range(16, 24):
                ada(q, q % 8, 16 * (q // 4 + 1), 2)
            product(0, 0, True)
            ga1 = mods_half[:, GA1, :]
            with dve.Fori(1, 7) as i:
                mod(i + 1, i + 1)
                dve.wait_ge(s_mods, 2 * i + 4)
                add_down(0, i, ga1)
                for m in range(8):
                    ada(8 * (i + 2) + m, m, 16 * (2 * i + 5 + m // 4), i + 2)
                product(0, i)
            mod(8, 8)
            with dve.Fori(7, NF) as i:
                add_down(0, i, ga1)
                product(0, i)
            def add_and_square(k, s, base, gate, low_banks):
                for j in range(16):
                    dve.wait_ge(s["down"], base + j + 1)
                    xs = x[:, j // 2, halves(j % 2)]
                    dve.scalar_tensor_tensor(xs, low_banks[j % len(low_banks)], gate[:, j // 2:j // 2 + 1], xs, ALU.mult,
                                             ALU.add).then_inc(s["x"], 1)
                    if j >= 3:
                        square_lo(k, j - 3)
                for j in range(13, 16):
                    square_lo(k, j)
                reciprocal(k, 0)
                reciprocal(k, 1)
            dve.wait_ge(fsem[0]["x"], 16 * (NF - 1) + 4)
            add_and_square(1, fsem[0], 16 * (NF - 1), ga1, ps_down)
            shift_scale(1)
            apply(1)

            def own(name, n, ins):
                ins.then_inc(q_[name], 1)
                dve.wait_ge(q_[name], n)

            def rotate(b, m, use, first=False):
                dve.wait_ge(psem["mm"][b], use + 1)
                n = m * 6 + (1 - b) * 3 + 2
                dve.stream_shuffle(rope_w, mix_ps[b], SWAP).then_inc(q_["w"], 1)
                dve.tensor_tensor(rt_f[b], mix_ps[b], rope_c, ALU.mult).then_inc(q_["w"], 1)
                dve.wait_ge(q_["w"], n + 2)
                dve.tensor_tensor(rope_w, rope_w, rope_s, ALU.mult).then_inc(q_["w"], 1)
                dve.wait_ge(q_["w"], n + 3)
                dve.tensor_tensor(rt_f[b], rt_f[b], rope_w, ALU.add).then_inc(psem["rt"][b], 1)

            def low(b, n, source, factor=1.0):
                dve.wait_ge(psem["qh"][b], n + 1)
                dve.scalar_tensor_tensor(q_lo[b], source, factor, q_hi[b].bitcast(F32), ALU.mult, ALU.subtract).then_inc(psem["ql"][b], 1)

            def blocks(kv):
                dve.wait_ge(psem["pair"][kv], 64)
                if kv == 0:
                    dve.memset(blk_f[:, :, :, N_CMP:N_CMP + 1], 0.0).then_inc(q_["blk"], 1)
                else:
                    dve.wait_ge(q_["bl"], 1)
                for g in range(2):
                    tokens = pairs[kv][g].rearrange("p (c s) -> p s c", s=16)
                    for part in range(2):
                        j = slice(8 * part, 8 * part + 8)
                        dve.tensor_tensor(blk_f[:, j, g, 0:N_CMP], tokens[:, 0:16:2, part:part + N_CMP],
                                          pe2[:, kv, j].unsqueeze(2).to_broadcast([P, 8, N_CMP]), ALU.add).then_inc(q_["blk"], 1)

            def blocks_low(kv):
                dve.wait_ge(q_["bh"], kv + 1)
                dve.tensor_tensor(rt(24, 2), ft(16, 2), rt(22, 2).bitcast(F32), ALU.subtract).then_inc(q_["bl"], 1)

            def hidden(kv):
                dve.wait_ge(q_["cmp"], chain("ha", kv))
                dve.tensor_tensor(hid_f[:], ps[:, 4, 0:P], hid_a[:], ALU.add).then_inc(q_["cmp"], 1)

            def hidden_t(kv):
                dve.wait_ge(q_["cmp"], chain("hh", kv))
                dve.tensor_tensor(hid_lo[:], ps[:, 5, 0:P], hid_hi[:].bitcast(F32), ALU.subtract).then_inc(q_["cmp"], 1)

            def compressed(kv):
                dve.wait_ge(q_["cmp"], chain("ch", kv))
                if kv == 0:
                    dve.tensor_tensor(kc_lo[:], ps[:, 4, 0:P], kc_hi[:].bitcast(F32), ALU.subtract).then_inc(q_["cmp"], 1)
                else:
                    dve.tensor_tensor(vc_st[:, HD:P], ps[:, 4, HD:P], vc_st[:, 0:HD].bitcast(F32), ALU.subtract).then_inc(q_["cmp"], 1)

            def log_forget():
                z, m, e, s, s2, a = (t[:] for t in lf)
                n = [0]

                def fl(ins):
                    n[0] += 1
                    own("fl", n[0], ins)
                dve.wait_ge(q_["fz"], 16)
                fl(dve.tensor_scalar(z, z, b_fg[:, 0:1], None, ALU.add))
                fl(dve.tensor_scalar(m, z, -1.0, None, ALU.mult))
                fl(dve.tensor_tensor(m, m, z, ALU.min))
                dve.wait_ge(q_["fe"], 1)
                fl(dve.tensor_scalar(s, e, 2.0, None, ALU.add))
                fl(dve.reciprocal(s, s))
                fl(dve.tensor_tensor(s, s, e, ALU.mult))
                fl(dve.tensor_tensor(s2, s, s, ALU.mult))
                for k, c in enumerate(LOG_COEFS):
                    if k == 0:
                        fl(dve.tensor_scalar(a, s2, c, None, ALU.mult))
                    else:
                        fl(dve.scalar_tensor_tensor(a, a, c, s2, ALU.add, ALU.mult))
                fl(dve.scalar_tensor_tensor(a, a, 1.0, s, ALU.add, ALU.mult))
                fl(dve.tensor_scalar(z, z, 0.0, None, ALU.min))
                fl(dve.scalar_tensor_tensor(s, a, -2.0, z, ALU.mult, ALU.add))
                assert n[0] == FL_STEPS

            def cumulate():
                c = rope_w[0:8, :]
                dve.wait_ge(q_["frow"], 16)
                dve.wait_ge(psem["rt"][0], 1)
                own("cf", 1, dve.tensor_tensor_scan(c, ft(16)[0:8, :], zero[0:8, 0:1].to_broadcast([8, T]), 0.0, ALU.add, ALU.min))
                own("cf", 2, dve.tensor_copy(cf_hi, c))
                own("cf", 3, dve.tensor_tensor(cf_lo, c, cf_hi.bitcast(F32), ALU.subtract))
                own("cf", 4, dve.tensor_scalar(ncf_hi, cf_hi.bitcast(F32), -1.0, None, ALU.mult))
                own("cf", 5, dve.tensor_scalar(ncf_lo, cf_lo.bitcast(F32), -1.0, None, ALU.mult))

            dve.wait_ge(q_["w2"], 1)
            dve.tensor_tensor(w2_lo[:], w2_f[:], w2_hi[:].bitcast(F32), ALU.subtract).then_inc(q_["w2"], 1)
            dve.wait_ge(q_["rope"], 3)
            dve.wait_ge(psem["mm"][0], 1)
            dve.stream_shuffle(rope_w, mix_ps[0], SWAP).then_inc(q_["w"], 1)
            dve.tensor_tensor(rt_f[0], mix_ps[0], rope_c, ALU.mult).then_inc(psem["free"][0], 1)
            dve.wait_ge(q_["w"], 1)
            dve.tensor_tensor(rope_w, rope_w, rope_s, ALU.mult).then_inc(q_["w"], 1)
            dve.wait_ge(q_["w"], 2)
            dve.wait_ge(psem["free"][0], 1)
            dve.tensor_tensor(rt_f[0], rt_f[0], rope_w, ALU.add).then_inc(psem["rt"][0], 1)
            blocks(0)
            blocks_low(0)
            hidden(0)
            log_forget()
            hidden_t(0)
            dve.wait_ge(q_["gtr"], 1)
            dve.tensor_copy(gate_t[:], ps_stat.rearrange("p (b m) -> p b m", b=NT)[:, :, 32:56]).then_inc(q_["gt"], 1)
            compressed(0)
            blocks(1)
            blocks_low(1)
            cumulate()
            hidden(1)
            dve.wait_ge(psem["st"][1], 128)
            rotate(1, 0, 11)
            low(1, 0, rt_f[1])
            hidden_t(1)
            dve.wait_ge(psem["st"][0], 128)
            rotate(0, 0, 12)
            low(0, 0, rt_f[0])
            compressed(1)
            for m in (1, 2):
                for b in (1, 0):
                    rotate(b, m, m + 12 - b)
                    low(b, m, rt_f[b], SCALE)
            with dve.Fori(0, 4) as m:
                for b in (1, 0):
                    low(b, m + 3, mix_ps[b], SCALE if b == 1 else 1.0)
            for n in range(6):
                dve.wait_ge(q_["vh"], n + 1)
                dve.tensor_tensor(v_st[:, :, :, HD:P], ps_v, v_st[:, :, :, 0:HD].bitcast(F32), ALU.subtract).then_inc(q_["vl"], 1)

            def attend(plan, a, it):
                n_rows, n_blocks, n_groups = plan.rows, len(plan.blocks), plan.groups

                def row_max(s):
                    dve.wait_ge(a["sd"], it * n_rows + (plan.row0 + s + 1))
                    dve.tensor_reduce(negmax[:, s % 8:s % 8 + 1], s_ps(s, plan.length(s)), AX.X, ALU.max, negate=True).then_inc(a["mx"], 1)

                def row_reciprocal(s):
                    dve.wait_ge(a["ex"], it * n_rows + (plan.row0 + s + 1))
                    dve.reciprocal(rinv[:, s % 8:s % 8 + 1], rowsum[:, s % 8:s % 8 + 1]).then_inc(a["ri"], 1)

                def low_part(b):
                    c = plan.first_row(b) * P
                    dve.wait_ge(a["ph"], it * n_blocks + (plan.block0 + b + 1))
                    dve.tensor_tensor(pt[b % 3][:, HALF + c:T], ps[:, 4 + b % 2, c:HALF], pt[b % 3][:, c:HALF].bitcast(F32),
                                      ALU.subtract).then_inc(a["pl"], 1)

                def o_add(og):
                    dve.wait_ge(a["oa"], it * n_groups + (plan.group0 + og + 1))
                    dve.tensor_tensor(o_sum, o_sum, ps[0:HD, 6 + og % 2, :], ALU.add).then_inc(a["oo"], 1)

                def o_low(og):
                    dve.wait_ge(a["oh"], it * n_groups + (plan.group0 + og + 1))
                    dve.tensor_tensor(o_st[:, HALF:T], o_sum, o_st[:, 0:HALF].bitcast(F32), ALU.subtract).then_inc(a["ol"], 1)

                for s in range(plan.steps):
                    if s < n_rows:
                        row_max(s)
                    for b in plan.at[s]:
                        low_part(b)
                        for og in plan.due(b, 4):
                            o_add(og)
                        for og in plan.due(b, 6):
                            o_low(og)
                    if 1 <= s <= n_rows:
                        row_reciprocal(s - 1)
                left = [(plan.last(og) + 4, o_add, og) for og in plan.left(4)] + [(plan.last(og) + 6, o_low, og) for og in plan.left(6)]
                for _, step, og in sorted(left, key=lambda e: e[0]):
                    step(og)

            dve.wait_ge(s_mask, 10)
            with dve.Fori(0, 2) as g:
                dve.tensor_copy(gate_g[:], gate_t[:, :, bass.ds(g * 12, 12)]).then_inc(s_gate, 1)
                attend(NSA, asem, g)
            with dve.Fori(0, 4) as p:
                attend(FOX, asem, p)

            def merge(m, first=False):
                s = osem
                for e, (done, load, up) in enumerate((("pa", "sga", "upa"), ("pb", "sgb", "up"))):
                    dve.wait_ge(s[up], m + 1)
                    dve.wait_ge(s[load], (m + 1) * 16)
                    if e == 0 and not first:
                        dve.wait_ge(s["act"], m)
                    dve.tensor_tensor(part[e], (ps_gate, ps_up)[e], sg[e], ALU.mult).then_inc(s[done], 1)
            merge(0, True)
            ga2 = mods[:, GA2, :]
            with dve.Fori(1, NT) as m:
                merge(m)
                add_down(OUT, m, ga2, ps_ring2)
            dve.wait_ge(osem["x"], 16 * (NT - 1) + 4)
            add_and_square(2, osem, 16 * (NT - 1), ga2, ps_down)
            shift_scale(2)
            apply(2)
            product(1, 0, True)
            ga3 = mods_half[:, GA3, :]
            with dve.Fori(1, NF) as i:
                add_down(1, i, ga3)
                product(1, i)
            dve.wait_ge(fsem[1]["x"], 16 * (NF - 1) + 4)
            add_and_square(3, fsem[1], 16 * (NF - 1), ga3, ps_down)
            for j in range(16):
                dve.wait_ge(nsem["rstd"], 2 * 3 + j % 2 + 1)
                xs = x[:, j // 2, halves(j % 2)]
                dve.scalar_tensor_tensor(xs, xs, gains[:, 3, j // 2:j // 2 + 1], rstd[:, halves(j % 2)], ALU.mult,
                                         ALU.mult).then_inc(s_fin, 1)

        @block.tensor
        def _(pe):
            def stat(k, j):
                s = nsem
                pe.wait_ge(s["lo"], 16 * k + j + 1)
                n, h = j // 2, j % 2
                pe.matmul(ps_stat[:, halves(h)], ones_r[:], sq_hi[:, j % 2, :], start=(n == 0), stop=False)
                pe.matmul(ps_stat[:, halves(h)], ones_r[:], sq_lo[:, j % 2, :], start=False,
                          stop=(n == NT - 1)).then_inc(s["mm"], 1)

            def product3(out, w, wl, m, ml, start, stop):
                pe.matmul(out, w, m, start=start, stop=False)
                pe.matmul(out, w, ml, start=False, stop=False)
                return pe.matmul(out, wl, m, start=False, stop=stop)

            def project(out, b, done, ready=None):
                wh = w_hi[b].rearrange("p (k m) -> p k m", k=NT)
                wl = w_lo[b].rearrange("p (k m) -> p k m", k=NT)
                for h in range(NH):
                    for k in range(NT):
                        if ready is not None:
                            pe.wait_ge(nsem["hl"], 16 * ready + h * NT + k + 1)
                        mm = product3(out[:, halves(h)], wh[:, k, :], wl[:, k, :], h_hi[:, k, halves(h)], h_lo[:, k, halves(h)],
                                      k == 0, k == NT - 1)
                mm.then_inc(done, 1)

            def mod_mm():
                for m in range(NT):
                    mm = pe.matmul(ps_stat[:, m:m + 1], ada_acc[:, m * P:(m + 1) * P], ones_f[:, 0:1], start=True, stop=True)
                mm.then_inc(s_mod_mm, 1)

            def down(f, i, ring=ps_down):
                s = fsem[f]
                pe.wait_ge(s["al"], i)
                pe.wait_ge(s["ld"], i)
                for k in range(16):
                    n, h = k // 2, k % 2
                    pe.wait_ge(s["x"], 16 * (i - 1) + k + 1)
                    product3(ring[k % 4], w_hi[DN][:, n * P:(n + 1) * P], w_lo[DN][:, n * P:(n + 1) * P],
                             act_hi[:, halves(h)], act_lo[:, halves(h)], True, True).then_inc(s["down"], 1)

            pe.wait_ge(s_const, 3)
            for j in range(16):
                stat(0, j)
            pe.wait_ge(nsem["std"], 2)
            pe.wait_ge(s_ada_used, 8)
            mod_mm()
            pe.wait_ge(s_ada_used, 16)
            pe.wait_ge(s_mods, 1)
            mod_mm()

            def ffn(f, norm, with_mods):
                s = fsem[f]
                pe.wait_ge(s["lg"], 1)
                project(ps_gate, G, s["gate"], norm)
                pe.wait_ge(s["lu"], 1)
                project(ps_up, U, s["up"])

                def body(i, mods_too):
                    pe.wait_ge(s["lg"], i + 1)
                    pe.wait_ge(s["silu"], i)
                    project(ps_gate, G, s["gate"])
                    if mods_too:
                        pe.wait_ge(s_ada_used, 8 * (i + 2))
                        pe.wait_ge(s_mods, 2 * i + 1)
                        mod_mm()
                    down(f, i)
                    pe.wait_ge(s["lu"], i + 1)
                    pe.wait_ge(s["x"], 16 * i + 2)
                    project(ps_up, U, s["up"])
                if with_mods:
                    with pe.Fori(1, 7) as i:
                        body(i, True)
                    pe.wait_ge(s_ada_used, 8 * 9)
                    pe.wait_ge(s_mods, 15)
                    mod_mm()
                with pe.Fori(7 if with_mods else 1, NF) as i:
                    body(i, False)

            def down_and_stats(s, i, norm, up_to):
                for k in range(16):
                    n, h = k // 2, k % 2
                    pe.wait_ge(s["x"], 16 * (i - 1) + k + 1)
                    product3(ps_down[k % 4], w_hi[DN][:, n * P:(n + 1) * P], w_lo[DN][:, n * P:(n + 1) * P],
                             act_hi[:, halves(h)], act_lo[:, halves(h)], True, True).then_inc(s["down"], 1)
                    if k >= 5:
                        stat(norm, k - 5)
                for k in range(11, 16):
                    stat(norm, k)

            def mix_tile(b, use, ready=None):
                pe.wait_ge(psem["wl"][b], use + 1)
                project(mix_ps[b], b, psem["mm"][b], ready)

            def compress(b, use, half):
                pe.wait_ge(psem["wl"][b], use + 1)
                w1 = rt(16 + 2 * b, 2).rearrange("p (s j m) -> p j s m", s=2, j=8)
                for j in range(8):
                    for k, part in enumerate((blk_hi, blk_lo)):
                        mm = pe.matmul(ps[:, 4, 0:2 * P], part[:, 8 * half + j, :], w1[:, j], start=(half + j + k == 0),
                                       stop=(half + j + k == 9))
                mm.then_inc(psem["mm"][b], 1)

            def hidden_transpose(kv):
                pe.wait_ge(q_["cmp"], chain("gel", kv))
                pe.transpose(ps[:, 5, 0:P], hid_f[:], ident_f[:]).then_inc(q_["cmp"], 1)

            def compress_out(kv):
                pe.wait_ge(q_["cmp"], chain("hl", kv))
                o = ps[:, 4, 0:P]
                if kv == 0:
                    mm = product3(o, w2_hi[:, 0, :], w2_lo[:, 0, :], hid_hi[:], hid_lo[:], True, True)
                else:
                    mm = product3(o, hid_hi[:], hid_lo[:], w2_hi[:, 1, :], w2_lo[:, 1, :], True, True)
                mm.then_inc(q_["cmp"], 1)

            def v_transposes(b, n):
                pe.wait_ge(psem["rt"][b], n // 2 + 13)
                if n >= 1:
                    pe.wait_ge(q_["vl"], n)
                for t in range(NT):
                    mm = pe.transpose(ps_v[:, t].rearrange("p h d -> p (h d)"), rt_f[b][:, t * P:(t + 1) * P], ident_f[:])
                mm.then_inc(q_["vtr"], 1)

            ffn(0, 0, True)
            pe.wait_ge(fsem[0]["al"], NF)
            pe.wait_ge(fsem[0]["ld"], NF)
            pe.wait_ge(s_mods, 17)
            down_and_stats(fsem[0], NF, 1, 11)
            mix_tile(0, 0, 1)
            mix_tile(1, 0)
            pe.wait_ge(psem["free"][0], 1)
            mix_tile(0, 1)
            pe.wait_ge(q_["bl"], 1)
            compress(1, 1, 0)
            compress(0, 2, 1)
            pe.wait_ge(psem["free"][0], 2)
            for t in range(NT):
                mm = pe.transpose(ps_stat[:, t * P:(t + 1) * P], rt_f[0][:, t * P:(t + 1) * P], ident_f[:])
            mm.then_inc(q_["gtr"], 1)
            pe.wait_ge(psem["rt"][1], 1)
            mix_tile(1, 2)
            hidden_transpose(0)
            pe.wait_ge(psem["free"][0], 2)
            mix_tile(0, 3)
            pe.wait_ge(q_["w2"], 2)
            compress_out(0)
            with pe.Fori(1, 8) as m:
                pe.wait_ge(psem["rt"][1], m + 1)
                mix_tile(1, m + 2)
                pe.wait_ge(psem["rt"][0], m + 1)
                mix_tile(0, m + 3)
            pe.wait_ge(q_["bl"], 2)
            pe.wait_ge(q_["cmp"], chain("cl", 0))
            compress(1, 10, 0)
            compress(0, 11, 1)
            pe.wait_ge(psem["rt"][1], 9)
            mix_tile(1, 11)
            hidden_transpose(1)
            pe.wait_ge(psem["rt"][0], 9)
            mix_tile(0, 12)
            compress_out(1)
            with pe.Fori(1, 3) as m:
                for b in (1, 0):
                    pe.wait_ge(psem["rt"][b], m + 9)
                    mix_tile(b, m + 12 - b)
            with pe.Fori(0, 4) as m:
                for b in (1, 0):
                    pe.wait_ge(psem["ql"][b], m + 3)
                    mix_tile(b, m + 15 - b)
            for n in range(6):
                b = 1 - n % 2
                if n < 2:
                    pe.wait_ge(psem["ql"][b], 7)
                else:
                    pe.wait_ge(psem["rt"][b], n // 2 + 12)
                mix_tile(b, n // 2 + 19 - b)
                if n >= 1:
                    v_transposes(n % 2, n - 1)
            v_transposes(0, 5)

            def scores(plan, a, it, s, operands, masked):
                n, at = plan.length(s), s_at(plan.length(s))
                if s >= 2:
                    pe.wait_ge(a["ex"], it * plan.rows + (plan.row0 + s - 1))
                q, q2, k1, k2, k_at = operands
                bank0 = 2 * (s % 2)
                for bank in range(2):
                    lo, hi = max(at, bank * HALF), min(at + n * P, (bank + 1) * HALF)
                    if lo >= hi:
                        continue
                    out = ps[:, bank0 + bank, lo - bank * HALF:hi - bank * HALF]
                    here = [(m, c) for m, c in masked if lo <= at + c * P < hi]
                    keys = slice(k_at + lo - at, k_at + hi - at)
                    pe.matmul(out, q, k1[:, keys], start=True, stop=False)
                    mm = pe.matmul(out, q2, k2[:, keys], start=False, stop=not here)
                    for m, c in here:
                        o = at + c * P - bank * HALF
                        mm = pe.matmul(ps[:, bank0 + bank, o:o + P], ident_b, m, start=False, stop=(m, c) == here[-1])
                mm.then_inc(a["sd"], 1)

            def transpose_block(plan, a, it, b):
                u, j = plan.blocks[b]
                if b == plan.first[u]:
                    pe.wait_ge(a["sc"], it * plan.rows + (plan.row0 + 4 * (u + 1)))
                if b >= 2:
                    pe.wait_ge(a["pl"], it * len(plan.blocks) + (plan.block0 + b - 1))
                for r in range(plan.first_row(b), 4):
                    mm = pe.transpose(ps[:, 4 + b % 2, r * P:(r + 1) * P], p_ring[(4 * u + r) % 8][:, j * P:(j + 1) * P], ident_f[:])
                mm.then_inc(a["tr"], 1)

            def values(plan, a, it, b, v):
                c = plan.first_row(b) * P
                og = plan.group(b)
                if plan.starts(b):
                    pe.wait_ge(a["oo"], it * plan.groups + (plan.group0 + og + 1))
                pe.wait_ge(a["pl"], it * len(plan.blocks) + (plan.block0 + b + 1))
                out = ps[:, 6 + og % 2, c:HALF]
                pe.matmul(out, v, pt[b % 3][:, c:HALF], start=plan.starts(b), stop=False)
                pe.matmul(out, v, pt[b % 3][:, HALF + c:T], start=False, stop=b == plan.last(og)).then_inc(a["pv"], 1)

            def attend(plan, a, it, score_row, value_tile):
                for s in range(plan.steps):
                    if s < plan.rows:
                        score_row(s)
                    for b in plan.at[s]:
                        transpose_block(plan, a, it, b)
                        if b >= 2:
                            values(plan, a, it, b - 2, value_tile(b - 2))
                for b in range(len(plan.blocks) - 2, len(plan.blocks)):
                    values(plan, a, it, b, value_tile(b))

            pe.wait_ge(q_["vl"], 6)
            pe.wait_ge(s_mask, 9)
            with pe.Fori(0, 2) as g:
                def score_row(s):
                    i, br = NSA_UNITS[s // 4]
                    if s == 0:
                        pe.wait_ge(s_nq, (g + 1) * 128)
                    if s // 4 in (SLC, WIN) and s % 4 == 0:
                        pe.wait_ge(s_nk[s // 4], (g + 1) * 64)
                    q = q_n[s % 4][:, i * P:(i + 1) * P]
                    if br == CMP:
                        m = [(cmp_mask[:, bass.ds(g * T + i * P, P)], 0)]
                        scores(NSA, asem, g, s, (q, q, kc_hi, kc_lo, 0), m)
                        return
                    n = NSA.length(s)
                    m = [(causal, n - 1)]
                    if br == WIN and i >= WIN_TILES:
                        m = [(far_edge, 0)] + m
                    scores(NSA, asem, g, s, (q, q, k1_n[br], k2_n[br], (i + 1 - n) * P), m)

                def value_tile(b):
                    u, j = NSA.blocks[b]
                    i, br = NSA_UNITS[u]
                    if br == CMP:
                        return vc_st[:]
                    if u == SLC:
                        pe.wait_ge(s_nv, (g + 1) * 32)
                    j += i + 1 - NSA.length(4 * u)
                    return v_n[br][:, j * P:(j + 1) * P]
                attend(NSA, asem, g, score_row, value_tile)
            with pe.Fori(0, 4) as p:
                def score_row(s):
                    e, half = FOX_UNITS[s // 4]
                    if s % 8 == 0:
                        pe.wait_ge(s_fox[e], (p + 1) * 176)
                    cols = slice((4 * half + s % 4) * P, (4 * half + s % 4 + 1) * P)
                    scores(FOX, asem, p, s, (q1_f[e][:, cols], q2_f[e][:, cols], k1_f[e], k2_f[e], 0), [(causal, FOX.length(s) - 1)])

                def value_tile(b):
                    u, j = FOX.blocks[b]
                    return v_f[FOX_UNITS[u][0]][:, j * P:(j + 1) * P]
                attend(FOX, asem, p, score_row, value_tile)

            def up(m, first=False):
                s = osem
                wh = w_hi[U].rearrange("p (k m) -> p k m", k=NT)
                wl = w_lo[U].rearrange("p (k m) -> p k m", k=NT)
                pe.wait_ge(s["lu"], m + 1)
                for e in range(2):
                    if first:
                        pe.wait_ge((s_on, s_of)[e], 128)
                    else:
                        pe.wait_ge(s[("pa", "pb")[e]], m)
                    for h in range(NH):
                        for k in range(4 * e, 4 * e + 4):
                            mm = product3((ps_gate, ps_up)[e][:, halves(h)], wh[:, k, :], wl[:, k, :], o_hi[k][:, halves(h)],
                                          o_lo[k][:, halves(h)], k == 4 * e, k == 4 * e + 3)
                    mm.then_inc(s[("upa", "up")[e]], 1)

            up(0, True)
            with pe.Fori(1, NT) as m:
                up(m)
                down(OUT, m, ps_ring2)
            pe.wait_ge(osem["al"], NT)
            pe.wait_ge(osem["ld"], NT)
            down_and_stats(osem, NT, 2, 11)
            pe.wait_ge(fsem[1]["lg"], 1)
            ffn(1, 2, False)
            pe.wait_ge(fsem[1]["al"], NF)
            pe.wait_ge(fsem[1]["ld"], NF)
            down_and_stats(fsem[1], NF, 3, 11)


def layout(inputs):
    import numpy as np
    A = {k: np.asarray(v) for k, v in inputs.items()}
    cols = lambda w: np.ascontiguousarray(w.reshape(NT, P, -1, P).transpose(2, 1, 0, 3)).reshape(-1, P, D)
    out = {
        "xT": np.ascontiguousarray(A["x"][0].T).reshape(NT, P, T),
        "c": np.ascontiguousarray(A["c"].reshape(NT, P).T),
        "b_ada": np.ascontiguousarray(A["b_ada"][0].reshape(N_MOD, NT, P).transpose(2, 0, 1)),
        "gains": np.ascontiguousarray(np.stack([A["g_ffn1"][0], A["g_mix"][0], A["g_ffn2"][0], A["g_final"]]).reshape(4, NT, P).transpose(2, 0, 1)),
        "w_ada": A["w_ada"][0],
    }
    w = A["w_in"][0]
    sizes = (512,) + (128,) * 6 + (24, 512, 512, 512, 8, 1024, 1024)
    at = np.cumsum((0,) + sizes)
    q_n, k_c, v_c, k_s, v_s, k_w, v_w, g_n, q_f, k_f, v_f, f_l, g_a, g_b = (w[:, at[i]:at[i + 1]] for i in range(14))
    gate_cols = np.zeros((D, P), w.dtype)
    gate_cols[:, 0:8] = f_l
    gate_cols[:, 32:56] = g_n
    w1 = [A[n][0].reshape(2, 8, P, P).transpose(0, 2, 1, 3).reshape(2, P, D) for n in ("w1_ck", "w1_cv")]
    merge = np.stack([cols(g_a), cols(g_b)], 1).reshape(16, P, D)
    fox = np.stack([cols(q_f), cols(k_f)], 1).reshape(8, P, D)
    out["wmix"] = np.concatenate([cols(k_c), cols(v_c), cols(gate_cols), w1[0], merge, w1[1], cols(k_s), cols(k_w), cols(q_n),
                                  fox, cols(v_s), cols(v_w), cols(v_f)])
    out["pos"] = A["positions"][0]
    d = np.arange(P) % HD
    freq = np.float32(500000.0) ** (-np.arange(8, dtype=np.float32) / np.float32(8))
    out["rope_k"] = np.stack([np.where(d < 16, freq[d % 8], 0), np.where(d < 8, -1, np.where(d < 16, 1, 0))], 1).astype(np.float32)
    out["pe2"] = np.stack([A[n][0].reshape(16, P).T for n in ("pe_ck", "pe_cv")], 1)
    out["b_fg"] = np.repeat(A["b_forget"][0], 16)[:, None]
    out["w2"] = np.stack([np.concatenate([A[n][0]] * 2, 1) for n in ("w2_ck", "w2_cv")], 1)
    out["w_up"] = cols(np.concatenate([A["w_up_nsa"][0], A["w_up_fox"][0]]))
    out["w_o"] = A["w_o"][0].reshape(NT, P, D)
    out = {k: np.ascontiguousarray(v) for k, v in out.items()}
    for f in (1, 2):
        out[f"wg{f}"] = cols(A[f"w_gate{f}"][0])
        out[f"wu{f}"] = cols(A[f"w_up{f}"][0])
        out[f"wd{f}"] = A[f"w_down{f}"][0].reshape(NF, P, D)
    return out


def kernel(**inputs):
    import concourse.bacc as bacc
    import numpy as np
    from concourse.bass_utils import run_bass_kernel_spmd

    nc = bacc.Bacc("TRN2", target_bir_lowering=False, num_devices=1)
    arrays = {f"in_{k}": a for k, a in layout(inputs).items()}
    aps = {k[3:]: nc.dram_tensor(k, a.shape, mybir.dt.from_np(a.dtype), kind="ExternalInput").ap() for k, a in arrays.items()}
    out = nc.dram_tensor("outT", (NT, P, T), F32, kind="ExternalOutput").ap()
    build(nc, aps, {"outT": out})
    results = run_bass_kernel_spmd(nc, [arrays], core_ids=[0]).results[0]
    return np.ascontiguousarray(results["outT"].reshape(D, T).T).reshape(1, T, D)
```

```python
from contextlib import ExitStack

import concourse.bass as bass
from concourse import mybir

F32 = mybir.dt.float32
F32R = mybir.dt.float32r
BF16 = mybir.dt.bfloat16
I32 = mybir.dt.int32
ALU = mybir.AluOpType
ACT = mybir.ActivationFunctionType
AX = mybir.AxisListType

P = 128
D = 1024
T = 1024
NT = D // P
HALF = 512
NH = T // HALF
FF = 2816
NF = FF // P
EPS = 1e-6
N_MOD = 9
HD = 64
N_CMP = 63
SCALE = HD ** -0.5
SEQ_TILES = 43
LOG_COEFS = tuple(1.0 / k for k in range(17, 1, -2))
FL_STEPS = 3 + 4 + len(LOG_COEFS) + 3
TWO_PI_PARTS = (6.28125, 0.0019350051879882812, 3.0199157663446274e-07)
SWAP = [(k + 8) % 16 if k < 16 else k for k in range(32)]
ROUND = 12582912.0
SH1, SC1, GA1, SH2, SC2, GA2, SH3, SC3, GA3 = range(N_MOD)


def halves(h):
    return slice(h * HALF, (h + 1) * HALF)


LAG = 8
RING = 11


class Plan:

    def __init__(self, units, group_units, before=None, times=0):
        self.units = units
        self.rows = 4 * len(units)
        self.blocks = [(u, j) for u, lens in enumerate(units) for j in range(max(lens))]
        self.first = [sum(max(l) for l in units[:u]) for u in range(len(units) + 1)]
        self.groups = len(units) // group_units
        self.group_units = group_units
        self.row0, self.block0, self.group0 = (times * before.rows, times * len(before.blocks), times * before.groups) if before else (0, 0, 0)
        self.steps = self.rows + LAG
        self.at = [[] for _ in range(self.steps)]
        for u, lens in enumerate(units):
            n = max(lens)
            for k in range(4):
                self.at[4 * u + LAG + k] += range(self.first[u] + n * k // 4, self.first[u] + n * (k + 1) // 4)

        self.bank, self.freed, owner, at = [], [], [None] * 4, 0
        for s in range(self.rows):
            n = 1 if self.length(s) <= 4 else 2
            if at + n > 4:
                at = 0
            before = [o for o in owner[at:at + n] if o is not None]
            self.bank.append(at)
            self.freed.append(max(before) if before else None)
            owner[at:at + n] = [s] * n
            at = (at + n) % 4
        self.step = {b: t for t, bs in enumerate(self.at) for b in bs}

    def length(self, s):
        return self.units[s // 4][s % 4]

    def first_row(self, b):
        u, j = self.blocks[b]
        return next(r for r in range(4) if self.units[u][r] > j)

    def group(self, b):
        return self.blocks[b][0] // self.group_units

    def starts(self, b):
        return b == self.first[self.group(b) * self.group_units]

    def last(self, og):
        return self.first[(og + 1) * self.group_units] - 1

    def due(self, b, behind):
        return [og for og in range(self.groups) if self.last(og) + behind == b]

    def left(self, behind):
        return [og for og in range(self.groups) if self.last(og) + behind >= len(self.blocks)]


WIN_TILES = 512 // P
CMP, SLC, WIN = range(3)
NSA_UNITS = [(i, br) for i in range(NT) for br in range(3)]
NSA = Plan([[(1, i + 1, min(i, WIN_TILES) + 1)[br]] * 4 for i, br in NSA_UNITS], 3)
FOX_HEADS = 4
FOX_UNITS = [(h, G) for h in range(FOX_HEADS) for G in range(2)]
FOX = Plan([[4 * G + r + 1 for r in range(4)] for h, G in FOX_UNITS], 1, NSA, 2)
NEG = -1e30


def build(nc, aps, outs):
    ctx = ExitStack()
    with ctx:
        def sb(name, shape, dt=F32):
            return ctx.enter_context(nc.sbuf_tensor(name, shape, dt))

        def sem(name):
            return ctx.enter_context(nc.semaphore(name))

        KW = T
        r_arena = sb("r_arena", [P, (16 + 6 + 6) * KW], F32R)
        f_arena = sb("f_arena", [P, (8 + 3 + 10) * KW])

        def rt(at, n=1):
            return r_arena[:, at * KW:(at + n) * KW]

        def ft(at, n=1):
            return f_arena[:, at * KW:(at + n) * KW]

        h_hi = rt(0, 8).rearrange("p (n t) -> p n t", n=NT)
        h_lo = rt(8, 8).rearrange("p (n t) -> p n t", n=NT)
        w_hi = [rt(16 + 2 * b) for b in range(3)]
        w_lo = [rt(17 + 2 * b) for b in range(3)]
        x = ft(0, 8).rearrange("p (n t) -> p n t", n=NT)
        w_raw = [ft(8 + b) for b in range(3)]
        act_hi, act_lo = rt(22), rt(23)
        sq_hi = rt(24).rearrange("p (r t) -> p r t", r=2)
        sq_lo = rt(25).rearrange("p (r t) -> p r t", r=2)
        silu_g, act_f = ft(11), ft(12)
        ada_raw = ft(13, 4).rearrange("p (r t) -> p r t", r=4)
        ada_acc = ft(17)
        sq_f = ft(18).rearrange("p (r t) -> p r t", r=2)
        nrm_u = sq_f
        nrm_t = ft(20).rearrange("p (r t) -> p r t", r=2)
        rstd = ft(19)
        gains = sb("gains_sb", [P, 4, NT])
        b_ada = sb("b_ada_sb", [P, N_MOD, NT])
        mods = sb("mods", [P, N_MOD, NT])
        mods_half = sb("mods_half", [P, N_MOD, NT])
        c_raw = sb("c_raw", [P, NT])
        c_act = sb("c_act", [P, NT])
        nrm_a = sb("nrm_a", [P, 3, NT])
        nrm_s = sb("nrm_s", [P, 3, NT])
        ones_f = sb("ones_f", [P, P])
        ones_r = sb("ones_r", [P, P], F32R)
        eps = sb("eps", [P, 1])
        c_scratch = sb("c_scratch", [P, 1])
        c_scratch2 = sb("c_scratch2", [P, 1])

        ps = ctx.enter_context(nc.psum_tensor("ps", [P, 8, HALF], F32))
        ps_gate = ps[:, 0:2, :].rearrange("p a b -> p (a b)")
        ps_up = ps[:, 2:4, :].rearrange("p a b -> p (a b)")
        ps_down = [ps[:, 2 + k, :] for k in range(4)]
        ps_mod0, ps_mod1 = ps[:, 4, 0:NT], ps[:, 5, 0:NT]
        ps_stat = ps[:, 6:8, :].rearrange("p a b -> p (a b)")

        rt_f = [ft(11), ft(12)]
        rope_s, rope_c, rope_w = ft(13), ft(14), ft(15)
        blk_f = ft(16, 2).rearrange("p (j g c) -> p j g c", j=16, g=2)
        pairs = [[ft(18), ft(19)], [ft(20), ft(10)]]
        q_hi, q_lo = [rt(22), rt(24)], [rt(23), rt(25)]
        blk_hi = rt(22, 2).rearrange("p (j m) -> p j m", j=16)
        blk_lo = rt(24, 2).rearrange("p (j m) -> p j m", j=16)
        v_st = rt(26, 2).rearrange("p (b h m) -> p b h m", b=NT, h=2)
        cf_hi, cf_lo, ncf_hi, ncf_lo = rt(20)[0:8], rt(21)[0:8], rt(20)[32:40], rt(21)[32:40]
        mix_ps = [ps_gate, ps_up]
        ps_v = ps[:, 4:6, :].rearrange("p a (b h d) -> p (a b) h d", h=2, d=HD)
        zero = sb("zero", [P, 1])
        ident_f = sb("ident_f", [P, P])
        gate_t = sb("gate_t", [P, NT, 24])
        rope_k = sb("rope_consts", [P, 2])
        pe2 = sb("pe2", [P, 2, 16])
        b_fg = sb("b_fg", [P, 1])
        w2_f = sb("w2_f", [P, 2, P])
        w2_hi = rt(26)[:, 0:2 * P].rearrange("p (k m) -> p k m", k=2)
        w2_lo = rt(26)[:, 2 * P:4 * P].rearrange("p (k m) -> p k m", k=2)
        hid_a = sb("hid_a", [P, P])
        hid_f = sb("hid_f", [P, P])
        hid_hi = rt(26)[:, 4 * P:5 * P]
        hid_lo = rt(26)[:, 5 * P:6 * P]
        kc_hi = sb("kc_hi", [P, P], F32R)
        kc_lo = sb("kc_lo", [P, P], F32R)
        vc_st = sb("vc_st", [P, P], F32R)
        lf = [sb(f"lf{i}", [P, HD]) for i in range(6)]

        q_n = [rt(22 + r) for r in range(4)]
        k1_n, k2_n, v_n = [None, rt(20), rt(4)], [None, rt(21), rt(5)], [None, rt(8), rt(9)]
        q1_f, q2_f, k1_f, k2_f, v_f = ([rt(a), rt(b)] for a, b in ((0, 7), (1, 14), (2, 15), (3, 16), (6, 17)))
        pt = [rt(10 + k) for k in range(3)]
        o_st = rt(13)[0:HD]
        p_ring = [ft(k) for k in (*range(11, 19), 8, 9, 10)]
        masks = ft(19, 2).bitcast(BF16)
        cmp_mask, causal, far_edge, ident_b = masks[:, 0:2048], masks[:, 2048:2176], masks[:, 2176:2304], masks[:, 2304:2432]
        o_sum = ft(20)[0:HD, HALF:T]
        negmax = sb("negmax", [P, RING])
        rowsum = sb("rowsum", [P, RING])
        rinv = sb("rinv", [P, RING])
        gate_g = sb("gate_g", [P, NT, 12])
        o_hi = [rt(k) for k in (4, 5, 8, 9, 0, 2, 6, 14)]
        o_lo = [rt(k) for k in (24, 25, 26, 27, 1, 3, 7, 15)]
        sg = [ft(13), ft(14)]
        part = [ft(15), ft(16)]
        wd_last, act_last = (rt(12), rt(13)), (rt(10), rt(11))
        ps_ring2 = [ps[:, 4 + k, :] for k in range(4)]

        def scratch(name, shape, dt=F32):
            return nc.dram_tensor(name, shape, dt, kind="Internal").ap()
        qk_d = [scratch("qk_hi_d", (14, P, T)), scratch("qk_lo_d", (14, P, T))]
        v_d = scratch("v_d", (6, P, 2 * T))
        cf_d = scratch("cf_d", (4, 8, T))
        sg_d = scratch("sg_d", (16, P, T))
        o_d = scratch("o_d", (2, 8, P, T))
        o_heads = [o_d[k].rearrange("n (e d) t -> (n e) d t", e=2) for k in range(2)]

        s_small = sem("small_in")
        s_x = [sem(f"x_in{n}") for n in range(NT)]
        s_ada = [sem(f"ada_in{r}") for r in range(4)]
        s_ada_used = sem("ada_used")
        s_mod_mm = sem("mod_mm")
        s_mods = sem("mods_done")
        s_c = sem("c_act")
        s_const = sem("const")
        s_raw = [[sem(f"raw{f}{b}") for b in range(3)] for f in range(3)]
        s_out = sem("out_done")

        nsem = {n: sem(f"n_{n}") for n in ("sq", "hi", "lo", "mm", "std", "rstd", "u", "t", "hh", "hl", "ab", "lop")}

        def ffn_sems(f):
            return {n: sem(f"f{f}_{n}") for n in ("hg", "hu", "hd", "lg", "lu", "ld", "gate", "up", "down", "x", "silu", "act", "ah", "al")}
        fsem = [ffn_sems(f) for f in range(2)]
        OUT = 2
        osem = {n: sem(f"o_{n}") for n in ("hu", "hd", "lu", "ld", "upa", "up", "down", "x", "pa", "pb", "act", "ah", "al", "sga", "sgb")}
        fsem.append(osem)
        asem = {n: sem(f"a_{n}") for n in ("sd", "mx", "ex", "ri", "sc", "tr", "ph", "pl", "pv", "oa", "oo", "oh", "ol", "st")}
        s_nq, s_nk, s_nv = sem("nsa_q_in"), [None, sem("nsa_ks_in"), sem("nsa_kw_in")], sem("nsa_v_in")
        s_fox, s_fox_v = [sem("fox_in_a"), sem("fox_in_b")], [sem("fox_v_in_a"), sem("fox_v_in_b")]
        s_gate, s_mask, s_fill = sem("gate_g"), sem("masks"), sem("fill")
        s_on, s_of = sem("o_nsa_in"), [sem("o_fox_in"), sem("o_last_in")]
        s_fin = sem("final")
        s_taken = sem("rows_taken")

        psem = {n: [sem(f"p_{n}{b}") for b in range(2)] for n in
                ("raw", "wh", "wl", "mm", "free", "rt", "qh", "ql", "st", "pair")}
        q_ = {n: sem(f"q_{n}") for n in
              ("const", "w", "rope", "pos", "sin", "own", "blk", "bh", "bl", "w2", "cmp",
               "gsg", "gtr", "gt", "frow", "fz", "fl", "cf", "cfd", "vtr", "vh", "vl", "vst", "fe")}

        def chain(step, kv):
            steps = ("ha", "hs", "gel", "tr", "hh", "hl", "cm2", "ch", "cl")
            return len(steps) * kv + steps.index(step) + 1


        def s_at(n):
            return P if n == 5 else 0

        def s_ps(plan, s):
            n, bank = plan.length(s), plan.bank[s]
            return ps[:, bank:bank + (2 if n > 4 else 1), :].rearrange("p a b -> p (a b)")[:, s_at(n):s_at(n) + n * P]

        def low_done(e, k, j):
            e.wait_ge(nsem[("lo", "lop")[j % 2]], 8 * k + j // 2 + 1)

        block = ctx.enter_context(nc.Block())

        w_of = [(aps["wg1"], aps["wu1"], aps["wd1"]), (aps["wg2"], aps["wu2"], aps["wd2"]), (None, aps["w_up"], aps["w_o"])]
        G, U, DN = range(3)

        @block.sync
        def _(sp):
            sp.dma_start(c_raw[:], aps["c"]).then_inc(s_small, 16)
            sp.dma_start(b_ada[:], aps["b_ada"]).then_inc(s_small, 16)
            sp.dma_start(gains[:], aps["gains"]).then_inc(s_small, 16)
            for tile, name in ((rope_k, "rope_k"), (pe2, "pe2"), (b_fg, "b_fg"), (w2_f, "w2")):
                sp.dma_start(tile[:], aps[name]).then_inc(s_small, 16)
            def ada(q, j=None):
                j = q // NT if j is None else j
                sp.dma_start(ada_raw[:, q % 4, :],
                             aps["w_ada"][(q % NT) * P:(q % NT + 1) * P, bass.ds(j * D, D)]).then_inc(s_ada[q % 4], 16)

            def weight(f, b, k):
                sp.dma_start(w_raw[b], w_of[f][b][k]).then_inc(s_raw[f][b], 16)

            def ffn_loads(f, with_ada):
                s = fsem[f]
                for k in (1, 2):
                    sp.wait_ge(s["lg"], k)
                    weight(f, G, k)
                    sp.wait_ge(s["ld" if k == 2 else "lu"], 1)
                    if k == 1:
                        weight(f, U, 1)
                        for q in range(3 * NT - 4, 3 * NT) if with_ada else ():
                            sp.wait_ge(s_ada_used, q - 3)
                            ada(q)
                    else:
                        weight(f, DN, 1)
                        sp.wait_ge(s["lu"], 2)
                        weight(f, U, 2)

                def body(i, ada_too):
                    if ada_too:
                        for m in range(4):
                            sp.wait_ge(s_ada_used, 8 * i + 13 + m)
                            ada(m, i + 2)
                    sp.wait_ge(s["lg"], i + 2)
                    weight(f, G, i + 2)
                    sp.wait_ge(s["ld"], i + 1)
                    weight(f, DN, i + 1)
                    if ada_too:
                        for m in range(4, 8):
                            sp.wait_ge(s_ada_used, 8 * i + 13 + m)
                            ada(m, i + 2)
                    sp.wait_ge(s["lu"], i + 2)
                    weight(f, U, i + 2)

                if with_ada:
                    with sp.Fori(1, 7) as i:
                        body(i, True)
                with sp.Fori(7 if with_ada else 1, NF - 2) as i:
                    body(i, False)
                sp.wait_ge(s["ld"], NF - 1)
                weight(f, DN, NF - 1)

            for q in range(3 * NT - 4):
                if q < NT:
                    sp.dma_start(x[:, q, :], aps["xT"][q]).then_inc(s_x[q], 16)
                if q >= 4:
                    sp.wait_ge(s_ada_used, q - 3)
                ada(q)
                if q == 11:
                    weight(0, G, 0)
                if q == 15:
                    weight(0, U, 0)
                if q == 19:
                    weight(0, DN, 0)
            ffn_loads(0, True)

            def mix_weight(b, i):
                sp.dma_start(w_raw[b], aps["wmix"][2 * i + b]).then_inc(psem["raw"][b], 16)
            sp.wait_ge(fsem[0]["lg"], NF)
            mix_weight(0, 0)
            sp.wait_ge(fsem[0]["lu"], NF)
            mix_weight(1, 0)
            with sp.Fori(1, 21) as i:
                for b in range(2):
                    sp.wait_ge(psem["wl"][b], i)
                    mix_weight(b, i)
            sp.wait_ge(psem["wl"][0], 21)
            mix_weight(0, 21)

            a = asem
            sp.wait_ge(psem["wl"][1], 21)
            weight(OUT, U, 0)
            def nsa_queries_keys(g, branches=(SLC, WIN)):
                for r in range(4) if SLC in branches else ():
                    for k in range(2):
                        sp.dma_start(q_n[r][k * HD:(k + 1) * HD].bitcast(F32),
                                     qk_d[k][2 + 2 * g + r // 2, (r % 2) * HD:(r % 2 + 1) * HD]).then_inc(s_nq, 16)
                for br in branches:
                    for k, tile in enumerate((k1_n[br], k2_n[br])):
                        for e in range(2):
                            sp.dma_start(tile[e * HD:(e + 1) * HD].bitcast(F32),
                                         qk_d[k][br - 1, g * HD:(g + 1) * HD]).then_inc(s_nk[br], 16)

            def nsa_values(g):
                for br in (SLC, WIN):
                    sp.dma_start(v_n[br].bitcast(F32).rearrange("p (b m) -> p b m", b=NT),
                                 v_d[br - 1].rearrange("p (b h m) -> p b h m", b=NT, h=2)[:, :, g]).then_inc(s_nv, 16)

            def nsa_store(g, i):
                sp.wait_ge(a["ol"], g * NT + i + 1)
                for k in range(2):
                    sp.dma_start(o_heads[k][4 * g:4 * g + 4, :, i * P:(i + 1) * P].rearrange("h d t -> d h t"),
                                 o_st[:, halves(k)].bitcast(F32).rearrange("d (h t) -> d h t", h=4)).then_inc(a["st"], 16)
            for b in range(2):
                sp.wait_ge(psem["st"][b], 352)
            sp.wait_ge(q_["cfd"], 64)
            nsa_queries_keys(0, (SLC,))
            sp.wait_ge(psem["mm"][1], 21)
            sp.wait_ge(psem["mm"][0], 22)
            nsa_queries_keys(0, (WIN,))
            sp.wait_ge(q_["vst"], 48)
            nsa_values(0)

            def fox_load(e, p):
                rows = slice(e * HD, (e + 1) * HD)
                for tile, k, j in ((q1_f, 0, 6), (q2_f, 0, 6), (k2_f, 1, 7)):
                    sp.dma_start(tile[e][0:HD].bitcast(F32), qk_d[k][p * 2 + j, rows]).then_inc(s_fox[e], 16)
                sp.dma_start(q1_f[e][HD:P].bitcast(F32), qk_d[1][p * 2 + 6, rows]).then_inc(s_fox[e], 16)
                for k in range(2):
                    sp.dma_start(k1_f[e][k * HD:(k + 1) * HD].bitcast(F32), qk_d[0][p * 2 + 7, rows]).then_inc(s_fox[e], 16)
                for k in range(2):
                    sp.dma_start(q2_f[e][HD + k:HD + k + 1].bitcast(F32), cf_d[k, bass.ds(p * 2 + e, 1)]).then_inc(s_fox[e], 16)
                    sp.dma_start(k2_f[e][HD + 2 + k:HD + 3 + k].bitcast(F32),
                                 cf_d[2 + k, bass.ds(p * 2 + e, 1)]).then_inc(s_fox[e], 16)

            def fox_values(e, p):
                sp.dma_start(v_f[e].bitcast(F32).rearrange("p (b m) -> p b m", b=NT),
                             v_d[p + 2].rearrange("p (b h m) -> p b h m", b=NT, h=2)[:, :, e]).then_inc(s_fox_v[e], 16)
            sp.wait_ge(s_fill, 8)
            sp.wait_ge(q_["vst"], 96)
            for e in range(2):
                fox_load(e, 0)
                fox_values(e, 0)
            for i in range(NT - 1):
                nsa_store(0, i)
            sp.wait_ge(a["sd"], NSA.rows)
            nsa_queries_keys(1)
            sp.wait_ge(a["pv"], len(NSA.blocks))
            nsa_values(1)
            for i in range(NT - 1, 2 * NT):
                nsa_store(i // NT, i % NT)
            sp.wait_ge(a["pv"], 2 * len(NSA.blocks))

            def o_load(n, signal):
                for k, tile in enumerate((o_hi[n], o_lo[n])):
                    sp.dma_start(tile.bitcast(F32), o_d[k][n]).then_inc(signal, 16)

            def fox_store(p, e, half):
                sp.wait_ge(a["ol"], p * 4 + (FOX.group0 + 2 * e + half + 1))
                for k in range(2):
                    sp.dma_start(o_heads[k][bass.ds(p * 2 + (8 + e), 1), :, halves(half)].rearrange("h d t -> d (h t)"),
                                 o_st[:, halves(k)].bitcast(F32)).then_inc(a["st"], 16)

            pair_rows, pair_blocks = 16, FOX.first[4]

            def rows_done(p, e):
                sp.wait_ge(a["sd"], p * pair_rows + (FOX.row0 + (e + 1) * pair_rows // 2))

            def values_done(p, e):
                sp.wait_ge(a["pv"], p * pair_blocks + (FOX.block0 + (e + 1) * pair_blocks // 2))

            def pair(p):
                rows_done(p, 0)
                fox_load(0, p + 1)
                fox_store(p, 0, 0)
                values_done(p, 0)
                fox_values(0, p + 1)
                rows_done(p, 1)
                fox_load(1, p + 1)
                fox_store(p, 0, 1)
                fox_store(p, 1, 0)
                values_done(p, 1)
                fox_values(1, p + 1)
                fox_store(p, 1, 1)
            sp.wait_ge(a["st"], 32 * (2 * NT + 1))
            for p in range(3):
                pair(p)
                o_load(p, s_on)
            o_load(3, s_on)
            rows_done(3, 0)
            sp.wait_ge(a["st"], 32 * (2 * NT + 8 + 1))
            o_load(4, s_of[0])
            o_load(5, s_of[0])
            fox_store(3, 0, 0)
            values_done(3, 0)
            rows_done(3, 1)
            sp.wait_ge(a["st"], 32 * (2 * NT + 12 + 1))
            o_load(6, s_of[0])
            for e, half in ((0, 1), (1, 0), (1, 1)):
                fox_store(3, e, half)
            sp.wait_ge(a["st"], 32 * (2 * NT + 16 + 1))
            o_load(7, s_of[1])

            s = osem
            values_done(3, 1)

            def sg_load(e, m):
                sp.dma_start(sg[e], sg_d[m * 2 + e]).then_inc(s[("sga", "sgb")[e]], 16)
            sg_load(0, 0)
            sg_load(1, 0)
            weight(OUT, DN, 0)
            sp.wait_ge(psem["wl"][0], 22)
            weight(1, G, 0)
            with sp.Fori(1, NT) as m:
                sp.wait_ge(s["lu"], m)
                weight(OUT, U, m)
                sp.wait_ge(s["ld"], m)
                weight(OUT, DN, m)
                sp.wait_ge(s["pa"], m)
                sg_load(0, m)
                sp.wait_ge(s["pb"], m)
                sg_load(1, m)
            sp.wait_ge(s["lu"], NT)
            weight(1, U, 0)
            sp.wait_ge(s["ld"], NT)
            weight(1, DN, 0)
            ffn_loads(1, False)
            for j in range(16):
                sp.wait_ge(s_fin, j + 1)
                sp.dma_start(outs["outT"][j % NT, :, halves(j // NT)], x[:, j % NT, halves(j // NT)]).then_inc(s_out, 16)
            sp.wait_ge(s_out, 256)

        @block.scalar
        def _(act):
            act.wait_ge(s_small, 112)
            act.activation(c_act[:], c_raw[:], ACT.Silu).then_inc(s_c, 1)

            def square(k, j, ready):
                s = nsem
                ready(act, j)
                if j >= 2:
                    low_done(act, k, j - 2)
                act.activation(sq_f[:, j % 2, :], x[:, j % NT, halves(j // NT)], ACT.Square).then_inc(s["sq"], 1)

            def std(k, h):
                s = nsem
                act.wait_ge(s["mm"], 16 * k + NT * (h + 1))
                act.activation(rstd[:, halves(h)], ps_stat[:, halves(h)], ACT.Sqrt, bias=eps[:, 0:1],
                                   scale=1.0 / D).then_inc(s["std"], 1)

            def apply(k):
                s = nsem
                for m in range(NT * NH):
                    act.wait_ge(s["t"], 16 * k + m + 1)
                    act.copy(h_hi[:, m % NT, halves(m // NT)], nrm_t[:, m % 2, :]).then_inc(s["hh"], 1)

            def x_loaded(e, j):
                e.wait_ge(s_x[j % NT], 16)

            def ffn_hi(f, b, k):
                act.wait_ge(s_raw[f][b], 16 * (k + 1))
                act.copy(w_hi[b], w_raw[b]).then_inc(fsem[f][("hg", "hu", "hd")[b]], 1)

            def w_high(b, k):
                act.wait_ge(psem["raw"][b], 16 * (k + 1))
                act.copy(w_hi[b], w_raw[b]).then_inc(psem["wh"][b], 1)

            def silu(f, i, first=False):
                s = fsem[f]
                act.wait_ge(s["gate"], i + 1)
                if not first:
                    act.wait_ge(s["act"], i)
                act.activation(silu_g, ps_gate, ACT.Silu).then_inc(s["silu"], 1)

            def act_high(f, i):
                s = fsem[f]
                act.wait_ge(s["act"], i + 1)
                act.copy(act_hi, act_f).then_inc(s["ah"], 1)

            def ffn(f):
                s = fsem[f]
                silu(f, 0, True)
                ffn_hi(f, G, 1)
                if f == 1:
                    act.wait_ge(osem["down"], NT * 16)
                ffn_hi(f, DN, 0)
                act.wait_ge(s["up"], 1)
                ffn_hi(f, U, 1)
                act_high(f, 0)
                def body(i):
                    silu(f, i)
                    ffn_hi(f, G, i + 1)
                    act.wait_ge(s["down"], i * 16)
                    ffn_hi(f, DN, i)
                    act.wait_ge(s["up"], i + 1)
                    ffn_hi(f, U, i + 1)
                    act_high(f, i)
                if f == 0:
                    with act.Fori(1, 14) as i:
                        body(i)
                    for k, table in enumerate((rope_s, rope_c)):
                        act.wait_ge(q_["rope"], k + 1)
                        act.activation(table, table, ACT.Sin).then_inc(q_["sin"], 1)
                with act.Fori(14 if f == 0 else 1, NF - 1) as i:
                    body(i)
                i = NF - 1
                silu(f, i)
                if f == 0:
                    act.wait_ge(s["gate"], NF)
                    w_high(0, 0)
                act.wait_ge(s["down"], i * 16)
                ffn_hi(f, DN, i)
                act_high(f, i)
                if f == 0:
                    w_high(1, 0)

            def x_added(base, s):
                return lambda e, j: e.wait_ge(s, base + j + 1)

            def pair_up(kv, b):
                for g in range(2):
                    rows = rt_f[b][g * HD:(g + 1) * HD]
                    act.dma_start(pairs[kv][g][0:HD, :], rows).then_inc(psem["pair"][kv], 16)
                    act.dma_start(pairs[kv][g][HD:P, 0:T - 1], rows[:, 1:T]).then_inc(psem["pair"][kv], 16)

            def gm(b, m, use, first=False):
                act.wait_ge(psem["mm"][b], use + 1)
                if not first:
                    act.wait_ge(psem["st"][b], m * 16)
                act.activation(rt_f[b], mix_ps[b], ACT.Sigmoid).then_inc(psem["rt"][b], 1)
                w_high(b, use + 1)
                act.wait_ge(psem["rt"][b], m + 2)
                act.dma_start(sg_d[m * 2 + 1 - b], rt_f[b]).then_inc(psem["st"][b], 16)

            def blocks_high(kv):
                act.wait_ge(q_["blk"], 4 * kv + 5)
                if kv == 1:
                    act.wait_ge(psem["mm"][0], 3)
                act.copy(rt(22, 2), ft(16, 2)).then_inc(q_["bh"], 1)

            def hidden(kv):
                act.wait_ge(psem["mm"][0], (3, 12)[kv])
                act.copy(hid_a[:], ps[:, 4, P:2 * P]).then_inc(q_["cmp"], 1)
                act.wait_ge(q_["cmp"], chain("hs", kv))
                act.activation(hid_f[:], hid_f[:], ACT.Gelu_apprx_tanh).then_inc(q_["cmp"], 1)

            def hidden_t(kv):
                act.wait_ge(q_["cmp"], chain("tr", kv))
                act.copy(hid_hi[:], ps[:, 5, 0:P]).then_inc(q_["cmp"], 1)

            def compressed(kv):
                act.wait_ge(q_["cmp"], chain("cm2", kv))
                if kv == 0:
                    act.copy(kc_hi[:], ps[:, 4, 0:P]).then_inc(q_["cmp"], 1)
                else:
                    act.copy(vc_st[:, 0:HD], ps[:, 4, 0:HD]).then_inc(q_["cmp"], 1)

            def qk_store(b, n, j):
                act.wait_ge(psem["ql"][b], n + 1)
                act.dma_start(qk_d[0][j], q_hi[b].bitcast(F32)).then_inc(psem["st"][b], 16)
                act.dma_start(qk_d[1][j], q_lo[b].bitcast(F32)).then_inc(psem["st"][b], 16)

            def rope(b, m, use, factor):
                act.wait_ge(psem["rt"][b], m + 10)
                act.wait_ge(psem["st"][b], m * 32 + 128)
                act.activation(q_hi[b], rt_f[b], ACT.Copy, scale=factor).then_inc(psem["qh"][b], 1)
                w_high(b, use + 1)
                qk_store(b, m, m * 2 + 1 - b)

            def plain(b, m, use, factor):
                act.wait_ge(psem["mm"][b], use + 1)
                act.wait_ge(psem["st"][b], m * 32 + 224)
                act.activation(q_hi[b], mix_ps[b], ACT.Copy, scale=factor).then_inc(psem["qh"][b], 1)
                w_high(b, use + 1)
                qk_store(b, m + 3, m * 2 + 7 - b)

            def v_copy(b, m, use, more):
                act.wait_ge(psem["mm"][b], use + 1)
                act.copy(rt_f[b], mix_ps[b]).then_inc(psem["rt"][b], 1)
                if more:
                    w_high(b, use + 1)

            def v_high(n):
                act.wait_ge(q_["vtr"], n + 1)
                if n >= 1:
                    act.wait_ge(q_["vst"], 16 * n)
                act.copy(v_st[:, :, :, 0:HD], ps_v).then_inc(q_["vh"], 1)
                act.wait_ge(q_["vl"], n + 1)
                act.dma_start(v_d[n], rt(26, 2).bitcast(F32)).then_inc(q_["vst"], 16)

            def attend(plan, a, it):
                n_rows, n_blocks, n_groups = plan.rows, len(plan.blocks), plan.groups

                def exp(s):
                    length = plan.length(s)
                    act.wait_ge(a["mx"], it * n_rows + (plan.row0 + s + 1))
                    if s >= RING:
                        act.wait_ge(a["tr"], it * n_blocks + (plan.block0 + plan.first[(s - RING) // 4 + 1]))
                    act.activation(p_ring[s % RING][:, 0:length * P], s_ps(plan, s), ACT.Exp, bias=negmax[:, s % RING:s % RING + 1],
                                   accum_out=rowsum[:, s % RING:s % RING + 1]).then_inc(a["ex"], 1)

                def high(b):
                    c = plan.first_row(b) * P
                    act.wait_ge(a["tr"], it * n_blocks + (plan.block0 + b + 1))
                    if b >= 3:
                        act.wait_ge(a["pv"], it * n_blocks + (plan.block0 + b - 2))
                    act.copy(pt[b % 3][:, c:HALF], ps[:, 4 + b % 2, c:HALF]).then_inc(a["ph"], 1)

                def o_upper(og):
                    act.wait_ge(a["pv"], it * n_blocks + (plan.block0 + plan.last(og) + 1))
                    if og >= 1:
                        act.wait_ge(a["ol"], it * n_groups + (plan.group0 + og))
                    act.copy(o_sum, ps[HD:P, 6 + og % 2, :]).then_inc(a["oa"], 1)

                def o_high(og):
                    act.wait_ge(a["oo"], it * n_groups + (plan.group0 + og + 3))
                    act.wait_ge(a["st"], it * (32 * n_groups) + 32 * (plan.group0 + og + 1))
                    act.copy(o_st[:, 0:HALF], o_sum).then_inc(a["oh"], 1)

                for s in range(plan.steps):
                    if 1 <= s <= n_rows:
                        exp(s - 1)
                    for b in plan.at[s]:
                        high(b)
                        for og in plan.due(b, 3):
                            o_upper(og)
                        for og in plan.due(b, 5):
                            o_high(og)
                left = [(plan.last(og) + 3, o_upper, og) for og in plan.left(3)] + [(plan.last(og) + 5, o_high, og) for og in plan.left(5)]
                for _, step, og in sorted(left, key=lambda e: e[0]):
                    step(og)

            act.wait_ge(s_const, 3)
            for j in range(16):
                square(0, j, x_loaded)
                if j == 14:
                    std(0, 0)
            std(0, 1)
            ffn_hi(0, G, 0)
            ffn_hi(0, U, 0)
            apply(0)
            ffn(0)
            for j in range(16):
                square(1, j, x_added(4 + 16 * (NF - 1), fsem[0]["x"]))
                if j == 14:
                    std(1, 0)
            std(1, 1)
            apply(1)
            act.copy(w2_hi[:], w2_f[:]).then_inc(q_["w2"], 1)
            act.wait_ge(psem["mm"][0], 1)
            w_high(0, 1)
            act.wait_ge(psem["rt"][0], 1)
            pair_up(0, 0)
            act.wait_ge(psem["mm"][1], 1)
            act.copy(rt_f[1], mix_ps[1]).then_inc(psem["rt"][1], 1)
            w_high(1, 1)
            act.wait_ge(psem["rt"][1], 1)
            pair_up(1, 1)
            blocks_high(0)
            act.wait_ge(psem["mm"][0], 2)
            act.wait_ge(psem["pair"][0], 64)
            act.activation(rt_f[0], mix_ps[0], ACT.Sigmoid).then_inc(q_["gsg"], 1)
            w_high(0, 2)
            act.wait_ge(q_["gsg"], 1)
            act.copy(rt_f[0][0:8, :], mix_ps[0][0:8, :]).then_inc(psem["free"][0], 1)
            act.wait_ge(psem["free"][0], 2)
            act.dma_start(lf[0][:], rt_f[0][0:8, :]).then_inc(q_["fz"], 16)
            act.wait_ge(psem["mm"][1], 2)
            w_high(1, 2)
            act.wait_ge(psem["mm"][0], 3)
            w_high(0, 3)
            hidden(0)
            act.wait_ge(q_["fl"], 3)
            act.activation(lf[2][:], lf[1][:], ACT.Exp).then_inc(q_["fe"], 1)
            act.wait_ge(psem["pair"][1], 64)
            gm(1, 0, 2, first=True)
            hidden_t(0)
            act.wait_ge(q_["gtr"], 1)
            act.wait_ge(q_["fz"], 16)
            gm(0, 0, 3, first=True)
            compressed(0)
            gm(1, 1, 3)
            gm(0, 1, 4)
            blocks_high(1)
            with act.Fori(2, 8) as m:
                gm(1, m, m + 2)
                gm(0, m, m + 3)
            act.wait_ge(q_["bl"], 2)
            act.wait_ge(q_["fl"], FL_STEPS)
            act.dma_start(ft(16)[0:8, :], lf[3][:]).then_inc(q_["frow"], 16)
            act.wait_ge(psem["mm"][1], 11)
            w_high(1, 11)
            act.wait_ge(psem["mm"][0], 12)
            w_high(0, 12)
            hidden(1)
            act.wait_ge(q_["cf"], 5)
            for k, rows in enumerate((cf_hi, cf_lo, ncf_hi, ncf_lo)):
                act.dma_start(cf_d[k], rows.bitcast(F32)).then_inc(q_["cfd"], 16)
            rope(1, 0, 11, 1.0)
            hidden_t(1)
            rope(0, 0, 12, 1.0)
            compressed(1)
            with act.Fori(1, 3) as m:
                rope(1, m, m + 11, SCALE)
                rope(0, m, m + 12, SCALE)
            with act.Fori(0, 4) as m:
                plain(1, m, m + 14, SCALE)
                plain(0, m, m + 15, 1.0)
            for n in range(6):
                v_copy(1 - n % 2, n // 2, n // 2 + (18, 19)[n % 2], n < 4)
                if n == 5:
                    ffn_hi(OUT, U, 0)
                if n >= 1:
                    v_high(n - 1)
            v_high(5)
            act.wait_ge(osem["lu"], 1)
            with act.Fori(0, 2) as g:
                attend(NSA, asem, g)
            with act.Fori(0, 8 // FOX_HEADS) as p:
                attend(FOX, asem, p)
            s = osem
            act.wait_ge(s["upa"], 1)
            act.wait_ge(s["up"], 1)
            ffn_hi(OUT, U, 1)
            act_high(OUT, 0)
            ffn_hi(OUT, DN, 0)
            ffn_hi(1, G, 0)
            with act.Fori(1, NT - 1) as m:
                act.wait_ge(s["up"], m + 1)
                ffn_hi(OUT, U, m + 1)
                act.wait_ge(s["down"], m * 16)
                ffn_hi(OUT, DN, m)
                act_high(OUT, m)
            act.wait_ge(s_raw[OUT][DN], 16 * NT)
            act.copy(wd_last[0], w_raw[DN]).then_inc(s["hd"], 1)
            act.wait_ge(s["up"], NT)
            ffn_hi(1, U, 0)
            act.wait_ge(s["act"], NT)
            act.copy(act_last[0], act_f).then_inc(s["ah"], 1)
            for j in range(16):
                square(2, j, x_added(4 + 16 * (NT - 1), s["x"]))
                if j == 14:
                    std(2, 0)
            std(2, 1)
            apply(2)
            ffn(1)
            for j in range(16):
                square(3, j, x_added(4 + 16 * (NF - 1), fsem[1]["x"]))
                if j == 14:
                    std(3, 0)
            std(3, 1)

        @block.gpsimd
        def _(pool):
            pool.memset(ones_f[:], 1.0).then_inc(s_const, 1)
            pool.memset(eps[:], EPS).then_inc(s_const, 1)
            pool.wait_ge(s_const, 2)
            pool.tensor_copy(ones_r[:], ones_f[:]).then_inc(s_const, 1)
            pool.memset(zero[:], 0.0).then_inc(q_["const"], 1)
            pool.memset(ident_f[:], 0.0).then_inc(q_["const"], 1)
            pool.wait_ge(q_["const"], 2)
            pool.affine_select(out=ident_f[:], in_=ident_f[:], compare_op=ALU.not_equal, fill=1.0, base=0,
                               pattern=[[-1, P]], channel_multiplier=1).then_inc(q_["const"], 1)

            def square_hi(k, j):
                s = nsem
                pool.wait_ge(s["sq"], 16 * k + j + 1)
                if j >= 2:
                    pool.wait_ge(s["mm"], 16 * k + j - 1)
                pool.tensor_scalar(sq_hi[:, j % 2, :], sq_f[:, j % 2, :], 1.0, 1.0, ALU.mult, ALU.mult).then_inc(s["hi"], 1)
                if j % 2 == 1:
                    pool.wait_ge(s["hi"], 16 * k + j + 1)
                    pool.tensor_tensor(sq_lo[:, 1, :], sq_f[:, 1, :], sq_hi[:, 1, :].bitcast(F32), ALU.subtract).then_inc(s["lop"], 1)

            def apply(k):
                s = nsem
                pool.wait_ge(s["ab"], k + 1)
                for m in range(NT * NH):
                    n = m % NT
                    pool.wait_ge(s["u"], 16 * k + m + 1)
                    if m >= 2:
                        pool.wait_ge(s["hl"], 16 * k + m - 1)
                    pool.tensor_scalar(nrm_t[:, m % 2, :], nrm_u[:, m % 2, :], nrm_a[:, k, n:n + 1], nrm_s[:, k, n:n + 1],
                                       ALU.mult, ALU.add).then_inc(s["t"], 1)

            def ffn_lo(f, b, k):
                s = fsem[f]
                pool.wait_ge(s[("hg", "hu", "hd")[b]], k + 1)
                pool.tensor_tensor(w_lo[b], w_raw[b], w_hi[b].bitcast(F32), ALU.subtract).then_inc(s[("lg", "lu", "ld")[b]], 1)

            def w_low(b, k):
                pool.wait_ge(psem["wh"][b], k + 1)
                pool.tensor_tensor(w_lo[b], w_raw[b], w_hi[b].bitcast(F32), ALU.subtract).then_inc(psem["wl"][b], 1)

            ang, turns, part_f = ft(15), ft(16), ft(17)
            steps = [0]

            def own(ins):
                steps[0] += 1
                ins.then_inc(q_["own"], 1)
                pool.wait_ge(q_["own"], steps[0])

            def rope_angles():
                pool.wait_ge(s_mod_mm, N_MOD)
                pool.wait_ge(s_ada_used, N_MOD * NT)
                pool.dma_start(part_f.bitcast(I32), aps["pos"].partition_broadcast(P)).then_inc(q_["pos"], 16)
                pool.wait_ge(q_["pos"], 16)
                own(pool.tensor_copy(ang, part_f.bitcast(I32)))
                own(pool.tensor_scalar(ang, ang, rope_k[:, 0:1], 1.0, ALU.mult, ALU.mult))

            def rope_turns(k):
                own(pool.tensor_scalar(turns, ang, 0.15915494309189535, (0.0, 0.25)[k], ALU.mult, ALU.add))
                own(pool.tensor_scalar(turns, turns, 1.0, ROUND, ALU.mult, ALU.add))
                own(pool.tensor_scalar(turns, turns, 1.0, -ROUND, ALU.mult, ALU.add))

            def rope_reduce(k, n):
                r = (rope_s, rope_c)[k]
                own(pool.tensor_scalar(part_f, turns, -TWO_PI_PARTS[n], 1.0, ALU.mult, ALU.mult))
                own(pool.tensor_tensor(r, ang if n == 0 else r, part_f, ALU.add))

            def rope_bound(k):
                r = (rope_s, rope_c)[k]
                if k == 1:
                    own(pool.tensor_scalar(r, r, 1.0, 1.5707963267948966, ALU.mult, ALU.add))
                pool.tensor_scalar(r, r, 3.1415925, -3.1415925, ALU.min, ALU.max).then_inc(q_["rope"], 1)

            def ffn(f):
                ffn_lo(f, G, 1)
                ffn_lo(f, DN, 0)
                ffn_lo(f, U, 1)

                def body(i, between=None):
                    for n, (b, k) in enumerate(((G, i + 1), (DN, i), (U, i + 1))):
                        ffn_lo(f, b, k)
                        if between is not None:
                            between(n)
                if f == 0:
                    with pool.Fori(1, 8) as i:
                        body(i)
                    body(8, lambda n: (rope_angles, lambda: rope_turns(0), lambda: rope_reduce(0, 0))[n]())
                    body(9, lambda n: (rope_reduce(0, n + 1) if n < 2 else rope_bound(0)))
                    body(10, lambda n: (rope_turns(1) if n == 0 else rope_reduce(1, n - 1)))
                    body(11, lambda n: (rope_reduce(1, 2) if n == 0 else rope_bound(1) if n == 1 else None))
                with pool.Fori(12 if f == 0 else 1, NF - 1) as i:
                    body(i)
                if f == 0:
                    w_low(0, 0)
                ffn_lo(f, DN, NF - 1)
                if f == 0:
                    w_low(1, 0)
                    pool.wait_ge(q_["sin"], 2)
                    pool.tensor_scalar(rope_s, rope_s, rope_k[:, 1:2], 1.0, ALU.mult, ALU.mult).then_inc(q_["rope"], 1)

            for j in range(16):
                square_hi(0, j)
            ffn_lo(0, G, 0)
            ffn_lo(0, U, 0)
            apply(0)
            ffn(0)
            for j in range(16):
                square_hi(1, j)

            apply(1)
            with pool.Fori(1, 21) as k:
                w_low(0, k)
                w_low(1, k)
            w_low(0, 21)

            def own(n, ins):
                ins.then_inc(s_mask, 1)
                pool.wait_ge(s_mask, n)
            pool.wait_ge(q_["blk"], 9)
            pool.wait_ge(q_["bl"], 2)
            own(1, pool.memset(cmp_mask, NEG))
            own(2, pool.memset(masks[:, 2048:2304], 0.0))
            for g in range(2):
                m = cmp_mask.rearrange("p (g i e c) -> p g i e c", g=2, i=NT, e=2)[:, g, :, g, :]
                own(3 + 2 * g, pool.memset(m, 0.0))
                own(4 + 2 * g, pool.affine_select(out=m, in_=m, compare_op=ALU.is_ge, fill=NEG, base=-31,
                                                  pattern=[[P, NT], [-16, HD]], channel_multiplier=1))
            own(7, pool.affine_select(out=causal, in_=causal, compare_op=ALU.is_ge, fill=NEG, base=0,
                                      pattern=[[-1, P]], channel_multiplier=1))
            own(8, pool.affine_select(out=far_edge, in_=far_edge, compare_op=ALU.is_ge, fill=NEG, base=-1,
                                      pattern=[[1, P]], channel_multiplier=-1))
            own(9, pool.tensor_copy(ident_b, ident_f[:]))
            pool.wait_ge(q_["gt"], 1)
            own(10, pool.affine_select(out=gate_t[:, 0, 0:24:3], in_=gate_t[:, 0, 0:24:3], compare_op=ALU.is_ge, fill=0.0, base=-31,
                                       pattern=[[0, 8]], channel_multiplier=1))
            pool.wait_ge(psem["mm"][0], 22)
            pool.wait_ge(psem["mm"][1], 21)
            n = 0
            for tile in (q2_f[0], k2_f[0], q2_f[1], k2_f[1]):
                pool.memset(tile[HD:P].bitcast(F32), 0.0).then_inc(s_fill, 1)
                n += 2
                pool.wait_ge(s_fill, n - 1)
                pool.memset(tile[HD:HD + 4].bitcast(F32), 1.0).then_inc(s_fill, 1)

            pool.wait_ge(s_fill, 8)
            ffn_lo(OUT, U, 0)

            def low_after(plan, og):
                b = plan.last(og) + 6
                return plan.step[b] - 1 if b < len(plan.blocks) else plan.rows

            def attend(plan, a, it, gates=None):
                def o_low(og):
                    pool.wait_ge(a["oh"], it * plan.groups + (plan.group0 + og + 1))
                    pool.tensor_tensor(o_st[:, HALF:T], o_sum, o_st[:, 0:HALF].bitcast(F32), ALU.subtract).then_inc(a["ol"], 1)

                for s in range(plan.rows):
                    p = p_ring[s % RING][:, 0:plan.length(s) * P]
                    pool.wait_ge(a["ri"], it * plan.rows + (plan.row0 + s + 1))
                    pool.sem_inc(s_taken, 1)
                    pool.tensor_scalar(p, p, rinv[:, s % RING:s % RING + 1], 1.0 if gates is None else gates(s), ALU.mult,
                                       ALU.mult).then_inc(a["sc"], 1)
                    for og in range(plan.groups):
                        if low_after(plan, og) == s:
                            o_low(og)
                for og in range(plan.groups):
                    if low_after(plan, og) >= plan.rows:
                        o_low(og)

            def nsa_gates(s):
                i, br = NSA_UNITS[s // 4]
                c = (s % 4) * 3 + br
                return gate_g[:, i, c:c + 1]
            with pool.Fori(0, 2) as g:
                pool.wait_ge(s_gate, g + 1)
                attend(NSA, asem, g, nsa_gates)
            with pool.Fori(0, 8 // FOX_HEADS) as p:
                attend(FOX, asem, p)

            def merge(m, to=(act_hi, act_lo), first=False):
                s = osem
                pool.wait_ge(s["pa"], m + 1)
                pool.wait_ge(s["pb"], m + 1)
                if not first:
                    pool.wait_ge(s["al"], m)
                pool.tensor_tensor(act_f, part[0], part[1], ALU.add).then_inc(s["act"], 1)
                pool.wait_ge(s["ah"], m + 1)
                pool.tensor_tensor(to[1], act_f, to[0].bitcast(F32), ALU.subtract).then_inc(s["al"], 1)
            ffn_lo(OUT, U, 1)
            merge(0, first=True)
            ffn_lo(OUT, DN, 0)
            ffn_lo(1, G, 0)
            with pool.Fori(1, NT - 1) as m:
                ffn_lo(OUT, U, m + 1)
                ffn_lo(OUT, DN, m)
                merge(m)
            pool.wait_ge(osem["hd"], NT)
            pool.tensor_tensor(wd_last[1], w_raw[DN], wd_last[0].bitcast(F32), ALU.subtract).then_inc(osem["ld"], 1)
            ffn_lo(1, U, 0)
            merge(NT - 1, act_last)
            for j in range(16):
                square_hi(2, j)
            apply(2)
            ffn(1)
            for j in range(16):
                square_hi(3, j)

        @block.vector
        def _(dve):
            def square_lo(k, j):
                s = nsem
                dve.wait_ge(s["hi"], 16 * k + j + 1)
                dve.tensor_tensor(sq_lo[:, j % 2, :], sq_f[:, j % 2, :], sq_hi[:, j % 2, :].bitcast(F32),
                                  ALU.subtract).then_inc(s["lo"], 1)

            def reciprocal(k, h):
                s = nsem
                dve.wait_ge(s["std"], 2 * k + h + 1)
                dve.reciprocal(rstd[:, halves(h)], rstd[:, halves(h)]).then_inc(s["rstd"], 1)

            def shift_scale(k):
                s = nsem
                sh, sc = 3 * k + SH1, 3 * k + SC1
                dve.wait_ge(s_mods, 2 * (sc + 1))
                dve.tensor_copy(nrm_s[:, k, :], mods[:, sh, :]).then_inc(s_const, 1)
                dve.wait_ge(s_const, 4 + k)
                dve.scalar_tensor_tensor(nrm_a[:, k, :], mods[:, sc, :], 1.0, gains[:, k, :], ALU.add,
                                         ALU.mult).then_inc(s["ab"], 1)

            def apply(k):
                s = nsem

                def scaled(m):
                    dve.wait_ge(s["rstd"], 2 * k + m // NT + 1)
                    if m >= 2:
                        dve.wait_ge(s["t"], 16 * k + m - 1)
                    dve.tensor_tensor(nrm_u[:, m % 2, :], x[:, m % NT, halves(m // NT)], rstd[:, halves(m // NT)],
                                      ALU.mult).then_inc(s["u"], 1)
                low_done(dve, k, 15)
                scaled(0)
                for m in range(NT * NH):
                    if m + 1 == NT:
                        reciprocal(k, 1)
                    if m + 1 < NT * NH:
                        scaled(m + 1)
                    dve.wait_ge(s["hh"], 16 * k + m + 1)
                    h = (slice(None), m % NT, halves(m // NT))
                    dve.tensor_tensor(h_lo[h], nrm_t[:, m % 2, :], h_hi[h].bitcast(F32), ALU.subtract).then_inc(s["hl"], 1)

            def ada(q, m, used, first_wait=None):
                dve.wait_ge(s_ada[m % 4], used)
                w = ada_raw[:, m % 4, :]
                if m == 0:
                    if first_wait is not None:
                        dve.wait_ge(s_mod_mm, first_wait)
                    dve.tensor_scalar(ada_acc, w, c_act[:, 0:1], None, ALU.mult).then_inc(s_ada_used, 1)
                else:
                    dve.wait_ge(s_ada_used, q)
                    dve.scalar_tensor_tensor(ada_acc, w, c_act[:, m:m + 1], ada_acc, ALU.mult, ALU.add).then_inc(s_ada_used, 1)

            def mod(j, n, out=ps_stat[:, 0:NT]):
                dve.wait_ge(s_mod_mm, n + 1)
                dve.tensor_tensor(mods[:, j, :], out, b_ada[:, j, :], ALU.add).then_inc(s_mods, 1)
                dve.wait_ge(s_mods, 2 * n + 1)
                dve.tensor_scalar(mods_half[:, j, :], mods[:, j, :], 0.5, None, ALU.mult).then_inc(s_mods, 1)

            def add_down(f, i, gate, ring=ps_down):
                s = fsem[f]
                dve.wait_ge(s["x"], 16 * (i - 1) + 4)
                for k in range(16):
                    n = k // 2
                    dve.wait_ge(s["down"], 16 * (i - 1) + k + 1)
                    xs = x[:, n, halves(k % 2)]
                    dve.scalar_tensor_tensor(xs, ring[k % 4], gate[:, n:n + 1], xs, ALU.mult, ALU.add).then_inc(s["x"], 1)

            def product(f, i, first=False):
                s = fsem[f]
                dve.wait_ge(s["up"], i + 1)
                dve.wait_ge(s["silu"], i + 1)
                if not first:
                    dve.wait_ge(s["al"], i)
                dve.tensor_tensor(act_f, silu_g, ps_up, ALU.mult).then_inc(s["act"], 1)
                dve.wait_ge(s["ah"], i + 1)
                dve.tensor_tensor(act_lo, act_f, act_hi.bitcast(F32), ALU.subtract).then_inc(s["al"], 1)

            dve.memset(c_scratch[:], 0.0).then_inc(fsem[0]["x"], 4)
            dve.memset(c_scratch2[:], 0.0).then_inc(fsem[1]["x"], 4)
            for n, c in ((osem["x"], 4), (asem["oo"], 2), (asem["st"], 32)):
                dve.memset(sb(f"credit{n.name}", [P, 1])[:], 0.0).then_inc(n, c)
            dve.wait_ge(s_c, 1)
            for q in range(16):
                ada(q, q % 8, 16 * (q // 4 + 1), 1 if q >= 8 else None)
                if q % 2 == 0:
                    square_lo(0, q)
            reciprocal(0, 0)
            mod(SH1, 0, ps_mod0)
            mod(SC1, 1, ps_mod1)
            shift_scale(0)
            apply(0)
            product(0, 0, True)
            for q in range(16, 24):
                ada(q, q % 8, 16 * (q // 4 + 1), 2)
            ga1 = mods_half[:, GA1, :]
            with dve.Fori(1, 7) as i:
                mod(i + 1, i + 1)
                dve.wait_ge(s_mods, 2 * i + 4)
                add_down(0, i, ga1)
                for m in range(8):
                    ada(8 * (i + 2) + m, m, 16 * (2 * i + 5 + m // 4), i + 2)
                product(0, i)
            mod(8, 8)
            with dve.Fori(7, NF) as i:
                add_down(0, i, ga1)
                product(0, i)
            def add_and_square(k, s, base, gate):
                for j in range(16):
                    dve.wait_ge(s["down"], base + j + 1)
                    n = j % NT
                    xs = x[:, n, halves(j // NT)]
                    dve.scalar_tensor_tensor(xs, ps_down[j % 4], gate[:, n:n + 1], xs, ALU.mult, ALU.add).then_inc(s["x"], 1)
                    if j >= 3 and j % 2 == 1:
                        square_lo(k, j - 3)
                reciprocal(k, 0)
                square_lo(k, 14)
            dve.wait_ge(fsem[0]["x"], 16 * (NF - 1) + 4)
            add_and_square(1, fsem[0], 16 * (NF - 1), ga1)
            shift_scale(1)
            apply(1)

            def own(name, n, ins):
                ins.then_inc(q_[name], 1)
                dve.wait_ge(q_[name], n)

            def rotate(b, m, use, first=False):
                dve.wait_ge(psem["mm"][b], use + 1)
                n = m * 6 + (1 - b) * 3 + 2
                dve.stream_shuffle(rope_w, mix_ps[b], SWAP).then_inc(q_["w"], 1)
                dve.tensor_tensor(rt_f[b], mix_ps[b], rope_c, ALU.mult).then_inc(q_["w"], 1)
                dve.wait_ge(q_["w"], n + 2)
                dve.tensor_tensor(rope_w, rope_w, rope_s, ALU.mult).then_inc(q_["w"], 1)
                dve.wait_ge(q_["w"], n + 3)
                dve.tensor_tensor(rt_f[b], rt_f[b], rope_w, ALU.add).then_inc(psem["rt"][b], 1)

            def low(b, n, source, factor=1.0):
                dve.wait_ge(psem["qh"][b], n + 1)
                dve.scalar_tensor_tensor(q_lo[b], source, factor, q_hi[b].bitcast(F32), ALU.mult, ALU.subtract).then_inc(psem["ql"][b], 1)

            def blocks(kv):
                dve.wait_ge(psem["pair"][kv], 64)
                if kv == 0:
                    dve.memset(blk_f[:, :, :, N_CMP:N_CMP + 1], 0.0).then_inc(q_["blk"], 1)
                else:
                    dve.wait_ge(q_["bl"], 1)
                for g in range(2):
                    tokens = pairs[kv][g].rearrange("p (c s) -> p s c", s=16)
                    for part in range(2):
                        j = slice(8 * part, 8 * part + 8)
                        dve.tensor_tensor(blk_f[:, j, g, 0:N_CMP], tokens[:, 0:16:2, part:part + N_CMP],
                                          pe2[:, kv, j].unsqueeze(2).to_broadcast([P, 8, N_CMP]), ALU.add).then_inc(q_["blk"], 1)

            def blocks_low(kv):
                dve.wait_ge(q_["bh"], kv + 1)
                dve.tensor_tensor(rt(24, 2), ft(16, 2), rt(22, 2).bitcast(F32), ALU.subtract).then_inc(q_["bl"], 1)

            def hidden(kv):
                dve.wait_ge(q_["cmp"], chain("ha", kv))
                dve.tensor_tensor(hid_f[:], ps[:, 4, 0:P], hid_a[:], ALU.add).then_inc(q_["cmp"], 1)

            def hidden_t(kv):
                dve.wait_ge(q_["cmp"], chain("hh", kv))
                dve.tensor_tensor(hid_lo[:], ps[:, 5, 0:P], hid_hi[:].bitcast(F32), ALU.subtract).then_inc(q_["cmp"], 1)

            def compressed(kv):
                dve.wait_ge(q_["cmp"], chain("ch", kv))
                if kv == 0:
                    dve.tensor_tensor(kc_lo[:], ps[:, 4, 0:P], kc_hi[:].bitcast(F32), ALU.subtract).then_inc(q_["cmp"], 1)
                else:
                    dve.tensor_tensor(vc_st[:, HD:P], ps[:, 4, HD:P], vc_st[:, 0:HD].bitcast(F32), ALU.subtract).then_inc(q_["cmp"], 1)

            def log_forget():
                z, m, e, s, s2, a = (t[:] for t in lf)
                n = [0]

                def fl(ins):
                    n[0] += 1
                    own("fl", n[0], ins)
                dve.wait_ge(q_["fz"], 16)
                fl(dve.tensor_scalar(z, z, b_fg[:, 0:1], None, ALU.add))
                fl(dve.tensor_scalar(m, z, -1.0, None, ALU.mult))
                fl(dve.tensor_tensor(m, m, z, ALU.min))
                dve.wait_ge(q_["fe"], 1)
                fl(dve.tensor_scalar(s, e, 2.0, None, ALU.add))
                fl(dve.reciprocal(s, s))
                fl(dve.tensor_tensor(s, s, e, ALU.mult))
                fl(dve.tensor_tensor(s2, s, s, ALU.mult))
                for k, c in enumerate(LOG_COEFS):
                    if k == 0:
                        fl(dve.tensor_scalar(a, s2, c, None, ALU.mult))
                    else:
                        fl(dve.scalar_tensor_tensor(a, a, c, s2, ALU.add, ALU.mult))
                fl(dve.scalar_tensor_tensor(a, a, 1.0, s, ALU.add, ALU.mult))
                fl(dve.tensor_scalar(z, z, 0.0, None, ALU.min))
                fl(dve.scalar_tensor_tensor(s, a, -2.0, z, ALU.mult, ALU.add))
                assert n[0] == FL_STEPS

            def cumulate():
                c = rope_w[0:8, :]
                dve.wait_ge(q_["frow"], 16)
                dve.wait_ge(psem["rt"][0], 1)
                own("cf", 1, dve.tensor_tensor_scan(c, ft(16)[0:8, :], zero[0:8, 0:1].to_broadcast([8, T]), 0.0, ALU.add, ALU.min))
                own("cf", 2, dve.tensor_copy(cf_hi, c))
                own("cf", 3, dve.tensor_tensor(cf_lo, c, cf_hi.bitcast(F32), ALU.subtract))
                own("cf", 4, dve.tensor_scalar(ncf_hi, cf_hi.bitcast(F32), -1.0, None, ALU.mult))
                own("cf", 5, dve.tensor_scalar(ncf_lo, cf_lo.bitcast(F32), -1.0, None, ALU.mult))

            dve.wait_ge(q_["w2"], 1)
            dve.tensor_tensor(w2_lo[:], w2_f[:], w2_hi[:].bitcast(F32), ALU.subtract).then_inc(q_["w2"], 1)
            dve.wait_ge(q_["rope"], 3)
            dve.wait_ge(psem["mm"][0], 1)
            dve.stream_shuffle(rope_w, mix_ps[0], SWAP).then_inc(q_["w"], 1)
            dve.tensor_tensor(rt_f[0], mix_ps[0], rope_c, ALU.mult).then_inc(psem["free"][0], 1)
            dve.wait_ge(q_["w"], 1)
            dve.tensor_tensor(rope_w, rope_w, rope_s, ALU.mult).then_inc(q_["w"], 1)
            dve.wait_ge(q_["w"], 2)
            dve.wait_ge(psem["free"][0], 1)
            dve.tensor_tensor(rt_f[0], rt_f[0], rope_w, ALU.add).then_inc(psem["rt"][0], 1)
            blocks(0)
            blocks_low(0)
            hidden(0)
            log_forget()
            hidden_t(0)
            dve.wait_ge(q_["gtr"], 1)
            dve.tensor_copy(gate_t[:], ps_stat.rearrange("p (b m) -> p b m", b=NT)[:, :, 32:56]).then_inc(q_["gt"], 1)
            compressed(0)
            blocks(1)
            blocks_low(1)
            cumulate()
            hidden(1)
            dve.wait_ge(psem["st"][1], 128)
            rotate(1, 0, 11)
            low(1, 0, rt_f[1])
            hidden_t(1)
            dve.wait_ge(psem["st"][0], 128)
            rotate(0, 0, 12)
            low(0, 0, rt_f[0])
            compressed(1)
            for m in (1, 2):
                for b in (1, 0):
                    rotate(b, m, m + 12 - b)
                    low(b, m, rt_f[b], SCALE)
            with dve.Fori(0, 4) as m:
                for b in (1, 0):
                    low(b, m + 3, mix_ps[b], SCALE if b == 1 else 1.0)
            for n in range(6):
                dve.wait_ge(q_["vh"], n + 1)
                dve.tensor_tensor(v_st[:, :, :, HD:P], ps_v, v_st[:, :, :, 0:HD].bitcast(F32), ALU.subtract).then_inc(q_["vl"], 1)

            def attend(plan, a, it):
                n_rows, n_blocks, n_groups = plan.rows, len(plan.blocks), plan.groups

                def row_max(s):
                    dve.wait_ge(a["sd"], it * n_rows + (plan.row0 + s + 1))
                    dve.tensor_reduce(negmax[:, s % RING:s % RING + 1], s_ps(plan, s), AX.X, ALU.max, negate=True).then_inc(a["mx"], 1)

                def row_reciprocal(s):
                    dve.wait_ge(a["ex"], it * n_rows + (plan.row0 + s + 1))
                    dve.reciprocal(rinv[:, s % RING:s % RING + 1], rowsum[:, s % RING:s % RING + 1]).then_inc(a["ri"], 1)

                def low_part(b):
                    c = plan.first_row(b) * P
                    dve.wait_ge(a["ph"], it * n_blocks + (plan.block0 + b + 1))
                    dve.tensor_tensor(pt[b % 3][:, HALF + c:T], ps[:, 4 + b % 2, c:HALF], pt[b % 3][:, c:HALF].bitcast(F32),
                                      ALU.subtract).then_inc(a["pl"], 1)

                def o_add(og):
                    dve.wait_ge(a["oa"], it * n_groups + (plan.group0 + og + 1))
                    dve.tensor_tensor(o_sum, o_sum, ps[0:HD, 6 + og % 2, :], ALU.add).then_inc(a["oo"], 1)

                for s in range(plan.steps):
                    if s < n_rows:
                        row_max(s)
                    for b in plan.at[s]:
                        low_part(b)
                        for og in plan.due(b, 4):
                            o_add(og)
                    if 1 <= s <= n_rows:
                        row_reciprocal(s - 1)
                for og in plan.left(4):
                    o_add(og)

            dve.wait_ge(s_mask, 10)
            with dve.Fori(0, 2) as g:
                dve.tensor_copy(gate_g[:], gate_t[:, :, bass.ds(g * 12, 12)]).then_inc(s_gate, 1)
                attend(NSA, asem, g)
            with dve.Fori(0, 8 // FOX_HEADS) as p:
                attend(FOX, asem, p)

            def merge(m, first=False):
                s = osem
                for e, (done, load, up) in enumerate((("pa", "sga", "upa"), ("pb", "sgb", "up"))):
                    dve.wait_ge(s[up], m + 1)
                    dve.wait_ge(s[load], (m + 1) * 16)
                    if e == 0 and not first:
                        dve.wait_ge(s["act"], m)
                    dve.tensor_tensor(part[e], (ps_gate, ps_up)[e], sg[e], ALU.mult).then_inc(s[done], 1)
            merge(0, True)
            ga2 = mods[:, GA2, :]
            with dve.Fori(1, NT) as m:
                merge(m)
                add_down(OUT, m, ga2, ps_ring2)
            dve.wait_ge(osem["x"], 16 * (NT - 1) + 4)
            add_and_square(2, osem, 16 * (NT - 1), ga2)
            shift_scale(2)
            apply(2)
            product(1, 0, True)
            ga3 = mods_half[:, GA3, :]
            with dve.Fori(1, NF) as i:
                add_down(1, i, ga3)
                product(1, i)
            dve.wait_ge(fsem[1]["x"], 16 * (NF - 1) + 4)
            add_and_square(3, fsem[1], 16 * (NF - 1), ga3)
            for j in range(16):
                n, h = j % NT, j // NT
                if j == NT:
                    reciprocal(3, 1)
                dve.wait_ge(nsem["rstd"], 2 * 3 + h + 1)
                xs = x[:, n, halves(h)]
                dve.scalar_tensor_tensor(xs, xs, gains[:, 3, n:n + 1], rstd[:, halves(h)], ALU.mult,
                                         ALU.mult).then_inc(s_fin, 1)

        @block.tensor
        def _(pe):
            def stat(k, j):
                s = nsem
                low_done(pe, k, j)
                n, h = j % NT, j // NT
                pe.matmul(ps_stat[:, halves(h)], ones_r[:], sq_hi[:, j % 2, :], start=(n == 0), stop=False)
                pe.matmul(ps_stat[:, halves(h)], ones_r[:], sq_lo[:, j % 2, :], start=False,
                          stop=(n == NT - 1)).then_inc(s["mm"], 1)

            def product3(out, w, wl, m, ml, start, stop):
                pe.matmul(out, w, m, start=start, stop=False)
                pe.matmul(out, w, ml, start=False, stop=False)
                return pe.matmul(out, wl, m, start=False, stop=stop)

            def project(out, b, done, ready=None):
                wh = w_hi[b].rearrange("p (k m) -> p k m", k=NT)
                wl = w_lo[b].rearrange("p (k m) -> p k m", k=NT)
                for h in range(NH):
                    for k in range(NT):
                        if ready is not None:
                            pe.wait_ge(nsem["hl"], 16 * ready + h * NT + k + 1)
                        mm = product3(out[:, halves(h)], wh[:, k, :], wl[:, k, :], h_hi[:, k, halves(h)], h_lo[:, k, halves(h)],
                                      k == 0, k == NT - 1)
                mm.then_inc(done, 1)

            def project2(outs, bs, dones, ready):
                ws = [[w[b].rearrange("p (k m) -> p k m", k=NT) for w in (w_hi, w_lo)] for b in bs]

                def piece(e, h, k):
                    return product3(outs[e][:, halves(h)], ws[e][0][:, k, :], ws[e][1][:, k, :], h_hi[:, k, halves(h)],
                                    h_lo[:, k, halves(h)], k == 0, k == NT - 1)
                for k in range(NT):
                    pe.wait_ge(nsem["hl"], 16 * ready + k + 1)
                    piece(0, 0, k)
                    piece(1, 0, k)
                for k in range(NT):
                    pe.wait_ge(nsem["hl"], 16 * ready + NT + k + 1)
                    mm = piece(0, 1, k)
                mm.then_inc(dones[0], 1)
                for k in range(NT):
                    mm = piece(1, 1, k)
                mm.then_inc(dones[1], 1)

            def mod_mm(out=ps_stat):
                for m in range(NT):
                    mm = pe.matmul(out[:, m:m + 1], ada_acc[:, m * P:(m + 1) * P], ones_f[:, 0:1], start=True, stop=True)
                mm.then_inc(s_mod_mm, 1)

            def down(f, i, ring=ps_down):
                s = fsem[f]
                pe.wait_ge(s["al"], i)
                pe.wait_ge(s["ld"], i)
                for k in range(16):
                    n, h = k // 2, k % 2
                    pe.wait_ge(s["x"], 16 * (i - 1) + k + 1)
                    product3(ring[k % 4], w_hi[DN][:, n * P:(n + 1) * P], w_lo[DN][:, n * P:(n + 1) * P],
                             act_hi[:, halves(h)], act_lo[:, halves(h)], True, True).then_inc(s["down"], 1)

            pe.wait_ge(s_const, 3)
            for h, out in enumerate((ps_mod0, ps_mod1)):
                for j in range(8 * h, 8 * h + 8):
                    stat(0, j)
                pe.wait_ge(s_ada_used, 8 * (h + 1))
                mod_mm(out)
            pe.wait_ge(nsem["std"], 2)

            def ffn(f, norm, with_mods):
                s = fsem[f]
                pe.wait_ge(s["lg"], 1)
                pe.wait_ge(s["lu"], 1)
                project2((ps_gate, ps_up), (G, U), (s["gate"], s["up"]), norm)

                def body(i, mods_too):
                    pe.wait_ge(s["lg"], i + 1)
                    pe.wait_ge(s["silu"], i)
                    project(ps_gate, G, s["gate"])
                    if mods_too:
                        pe.wait_ge(s_ada_used, 8 * (i + 2))
                        pe.wait_ge(s_mods, 2 * i + 1)
                        mod_mm()
                    down(f, i)
                    pe.wait_ge(s["lu"], i + 1)
                    pe.wait_ge(s["x"], 16 * i + 2)
                    project(ps_up, U, s["up"])
                if with_mods:
                    with pe.Fori(1, 7) as i:
                        body(i, True)
                    pe.wait_ge(s_ada_used, 8 * 9)
                    pe.wait_ge(s_mods, 15)
                    mod_mm()
                with pe.Fori(7 if with_mods else 1, NF) as i:
                    body(i, False)

            def down_and_stats(s, i, norm, w=(w_hi[DN], w_lo[DN]), a=(act_hi, act_lo)):
                for k in range(16):
                    n, h = k % NT, k // NT
                    pe.wait_ge(s["x"], 16 * (i - 1) + k + 1)
                    product3(ps_down[k % 4], w[0][:, n * P:(n + 1) * P], w[1][:, n * P:(n + 1) * P],
                             a[0][:, halves(h)], a[1][:, halves(h)], True, True).then_inc(s["down"], 1)
                    if k >= 5:
                        stat(norm, k - 5)
                for k in range(11, 16):
                    stat(norm, k)

            def mix_tile(b, use, ready=None):
                pe.wait_ge(psem["wl"][b], use + 1)
                project(mix_ps[b], b, psem["mm"][b], ready)

            def compress(b, use, half):
                pe.wait_ge(psem["wl"][b], use + 1)
                w1 = rt(16 + 2 * b, 2).rearrange("p (s j m) -> p j s m", s=2, j=8)
                for j in range(8):
                    for k, part in enumerate((blk_hi, blk_lo)):
                        mm = pe.matmul(ps[:, 4, 0:2 * P], part[:, 8 * half + j, :], w1[:, j], start=(half + j + k == 0),
                                       stop=(half + j + k == 9))
                mm.then_inc(psem["mm"][b], 1)

            def hidden_transpose(kv):
                pe.wait_ge(q_["cmp"], chain("gel", kv))
                pe.transpose(ps[:, 5, 0:P], hid_f[:], ident_f[:]).then_inc(q_["cmp"], 1)

            def compress_out(kv):
                pe.wait_ge(q_["cmp"], chain("hl", kv))
                o = ps[:, 4, 0:P]
                if kv == 0:
                    mm = product3(o, w2_hi[:, 0, :], w2_lo[:, 0, :], hid_hi[:], hid_lo[:], True, True)
                else:
                    mm = product3(o, hid_hi[:], hid_lo[:], w2_hi[:, 1, :], w2_lo[:, 1, :], True, True)
                mm.then_inc(q_["cmp"], 1)

            def v_transposes(b, n):
                pe.wait_ge(psem["rt"][b], n // 2 + 13)
                if n >= 1:
                    pe.wait_ge(q_["vl"], n)
                for t in range(NT):
                    mm = pe.transpose(ps_v[:, t].rearrange("p h d -> p (h d)"), rt_f[b][:, t * P:(t + 1) * P], ident_f[:])
                mm.then_inc(q_["vtr"], 1)

            ffn(0, 0, True)
            pe.wait_ge(fsem[0]["al"], NF)
            pe.wait_ge(fsem[0]["ld"], NF)
            pe.wait_ge(s_mods, 17)
            down_and_stats(fsem[0], NF, 1)
            pe.wait_ge(psem["wl"][0], 1)
            pe.wait_ge(psem["wl"][1], 1)
            project2(mix_ps, (0, 1), (psem["mm"][0], psem["mm"][1]), 1)
            pe.wait_ge(psem["free"][0], 1)
            mix_tile(0, 1)
            pe.wait_ge(q_["bl"], 1)
            compress(1, 1, 0)
            compress(0, 2, 1)
            pe.wait_ge(psem["free"][0], 2)
            for t in range(NT):
                mm = pe.transpose(ps_stat[:, t * P:(t + 1) * P], rt_f[0][:, t * P:(t + 1) * P], ident_f[:])
            mm.then_inc(q_["gtr"], 1)
            pe.wait_ge(psem["rt"][1], 1)
            mix_tile(1, 2)
            hidden_transpose(0)
            pe.wait_ge(psem["free"][0], 2)
            mix_tile(0, 3)
            pe.wait_ge(q_["w2"], 2)
            compress_out(0)
            with pe.Fori(1, 8) as m:
                pe.wait_ge(psem["rt"][1], m + 1)
                mix_tile(1, m + 2)
                pe.wait_ge(psem["rt"][0], m + 1)
                mix_tile(0, m + 3)
            pe.wait_ge(q_["bl"], 2)
            pe.wait_ge(q_["cmp"], chain("cl", 0))
            compress(1, 10, 0)
            compress(0, 11, 1)
            pe.wait_ge(psem["rt"][1], 9)
            mix_tile(1, 11)
            hidden_transpose(1)
            pe.wait_ge(psem["rt"][0], 9)
            mix_tile(0, 12)
            compress_out(1)
            with pe.Fori(1, 3) as m:
                for b in (1, 0):
                    pe.wait_ge(psem["rt"][b], m + 9)
                    mix_tile(b, m + 12 - b)
            with pe.Fori(0, 4) as m:
                for b in (1, 0):
                    pe.wait_ge(psem["ql"][b], m + 3)
                    mix_tile(b, m + 15 - b)
            for n in range(6):
                b = 1 - n % 2
                if n < 2:
                    pe.wait_ge(psem["ql"][b], 7)
                else:
                    pe.wait_ge(psem["rt"][b], n // 2 + 12)
                mix_tile(b, n // 2 + 19 - b)
                if n >= 1:
                    v_transposes(n % 2, n - 1)
            v_transposes(0, 5)

            def scores(plan, a, it, s, operands, masked):
                n, at = plan.length(s), s_at(plan.length(s))
                if plan.freed[s] is not None:
                    pe.wait_ge(a["ex"], it * plan.rows + (plan.row0 + plan.freed[s] + 1))
                q, q2, k1, k2, k_at = operands
                bank0 = plan.bank[s]
                for bank in range(2):
                    lo, hi = max(at, bank * HALF), min(at + n * P, (bank + 1) * HALF)
                    if lo >= hi:
                        continue
                    out = ps[:, bank0 + bank, lo - bank * HALF:hi - bank * HALF]
                    here = [(m, c) for m, c in masked if lo <= at + c * P < hi]
                    keys = slice(k_at + lo - at, k_at + hi - at)
                    pe.matmul(out, q, k1[:, keys], start=True, stop=False)
                    mm = pe.matmul(out, q2, k2[:, keys], start=False, stop=not here)
                    for m, c in here:
                        o = at + c * P - bank * HALF
                        mm = pe.matmul(ps[:, bank0 + bank, o:o + P], ident_b, m, start=False, stop=(m, c) == here[-1])
                mm.then_inc(a["sd"], 1)

            def transpose_block(plan, a, it, b):
                u, j = plan.blocks[b]
                if b == plan.first[u]:
                    pe.wait_ge(a["sc"], it * plan.rows + (plan.row0 + 4 * (u + 1)))
                if b >= 2:
                    pe.wait_ge(a["pl"], it * len(plan.blocks) + (plan.block0 + b - 1))
                for r in range(plan.first_row(b), 4):
                    mm = pe.transpose(ps[:, 4 + b % 2, r * P:(r + 1) * P], p_ring[(4 * u + r) % RING][:, j * P:(j + 1) * P], ident_f[:])
                mm.then_inc(a["tr"], 1)

            def values(plan, a, it, b, v):
                c = plan.first_row(b) * P
                og = plan.group(b)
                if plan.starts(b):
                    pe.wait_ge(a["oo"], it * plan.groups + (plan.group0 + og + 1))
                pe.wait_ge(a["pl"], it * len(plan.blocks) + (plan.block0 + b + 1))
                out = ps[:, 6 + og % 2, c:HALF]
                pe.matmul(out, v, pt[b % 3][:, c:HALF], start=plan.starts(b), stop=False)
                pe.matmul(out, v, pt[b % 3][:, HALF + c:T], start=False, stop=b == plan.last(og)).then_inc(a["pv"], 1)

            def attend(plan, a, it, score_row, value_tile):
                for s in range(plan.steps):
                    if s < plan.rows:
                        score_row(s)
                    for b in plan.at[s]:
                        transpose_block(plan, a, it, b)
                        if b >= 2:
                            values(plan, a, it, b - 2, value_tile(b - 2))
                for b in range(len(plan.blocks) - 2, len(plan.blocks)):
                    values(plan, a, it, b, value_tile(b))

            pe.wait_ge(s_mask, 9)
            with pe.Fori(0, 2) as g:
                def score_row(s):
                    i, br = NSA_UNITS[s // 4]
                    if s == 0:
                        pe.wait_ge(s_nq, (g + 1) * 128)
                    if s == LAG - 1:
                        pe.wait_ge(q_["vl"], 6)
                    if s // 4 in (SLC, WIN) and s % 4 == 0:
                        pe.wait_ge(s_nk[s // 4], (g + 1) * 64)
                    q = q_n[s % 4][:, i * P:(i + 1) * P]
                    if br == CMP:
                        m = [(cmp_mask[:, bass.ds(g * T + i * P, P)], 0)]
                        scores(NSA, asem, g, s, (q, q, kc_hi, kc_lo, 0), m)
                        return
                    n = NSA.length(s)
                    m = [(causal, n - 1)]
                    if br == WIN and i >= WIN_TILES:
                        m = [(far_edge, 0)] + m
                    scores(NSA, asem, g, s, (q, q, k1_n[br], k2_n[br], (i + 1 - n) * P), m)

                def value_tile(b):
                    u, j = NSA.blocks[b]
                    i, br = NSA_UNITS[u]
                    if br == CMP:
                        return vc_st[:]
                    if u == SLC:
                        pe.wait_ge(s_nv, (g + 1) * 32)
                    j += i + 1 - NSA.length(4 * u)
                    return v_n[br][:, j * P:(j + 1) * P]
                attend(NSA, asem, g, score_row, value_tile)
            with pe.Fori(0, 8 // FOX_HEADS) as p:
                def score_row(s):
                    e, half = FOX_UNITS[s // 4]
                    if s % 8 == 0:
                        pe.wait_ge(s_fox[e % 2], p * (FOX_HEADS // 2 * 160) + (e // 2 + 1) * 160)
                    e %= 2
                    cols = slice((4 * half + s % 4) * P, (4 * half + s % 4 + 1) * P)
                    scores(FOX, asem, p, s, (q1_f[e][:, cols], q2_f[e][:, cols], k1_f[e], k2_f[e], 0), [(causal, FOX.length(s) - 1)])

                def value_tile(b):
                    u, j = FOX.blocks[b]
                    e, half = FOX_UNITS[u]
                    if half == 0 and j == 0:
                        pe.wait_ge(s_fox_v[e % 2], p * (FOX_HEADS // 2 * 16) + (e // 2 + 1) * 16)
                    return v_f[e % 2][:, j * P:(j + 1) * P]
                attend(FOX, asem, p, score_row, value_tile)

            def up(m, first=False):
                s = osem
                wh = w_hi[U].rearrange("p (k m) -> p k m", k=NT)
                wl = w_lo[U].rearrange("p (k m) -> p k m", k=NT)
                pe.wait_ge(s["lu"], m + 1)
                for e in range(2):
                    if first:
                        pe.wait_ge((s_on, s_of[0])[e], (128, 96)[e])
                    else:
                        pe.wait_ge(s[("pa", "pb")[e]], m)
                    for h in range(NH):
                        for k in range(4 * e, 4 * e + 4):
                            if first and k == NT - 1:
                                pe.wait_ge(s_of[1], 32)
                            mm = product3((ps_gate, ps_up)[e][:, halves(h)], wh[:, k, :], wl[:, k, :], o_hi[k][:, halves(h)],
                                          o_lo[k][:, halves(h)], k == 4 * e, k == 4 * e + 3)
                    mm.then_inc(s[("upa", "up")[e]], 1)

            up(0, True)
            with pe.Fori(1, NT) as m:
                up(m)
                down(OUT, m, ps_ring2)
            pe.wait_ge(osem["al"], NT)
            pe.wait_ge(osem["ld"], NT)
            down_and_stats(osem, NT, 2, wd_last, act_last)
            pe.wait_ge(fsem[1]["lg"], 1)
            ffn(1, 2, False)
            pe.wait_ge(fsem[1]["al"], NF)
            pe.wait_ge(fsem[1]["ld"], NF)
            down_and_stats(fsem[1], NF, 3)


def layout(inputs):
    import numpy as np
    A = {k: np.asarray(v) for k, v in inputs.items()}
    cols = lambda w: np.ascontiguousarray(w.reshape(NT, P, -1, P).transpose(2, 1, 0, 3)).reshape(-1, P, D)
    out = {
        "xT": np.ascontiguousarray(A["x"][0].T).reshape(NT, P, T),
        "c": np.ascontiguousarray(A["c"].reshape(NT, P).T),
        "b_ada": np.ascontiguousarray(A["b_ada"][0].reshape(N_MOD, NT, P).transpose(2, 0, 1)),
        "gains": np.ascontiguousarray(np.stack([A["g_ffn1"][0], A["g_mix"][0], A["g_ffn2"][0], A["g_final"]]).reshape(4, NT, P).transpose(2, 0, 1)),
        "w_ada": A["w_ada"][0],
    }
    w = A["w_in"][0]
    sizes = (512,) + (128,) * 6 + (24, 512, 512, 512, 8, 1024, 1024)
    at = np.cumsum((0,) + sizes)
    q_n, k_c, v_c, k_s, v_s, k_w, v_w, g_n, q_f, k_f, v_f, f_l, g_a, g_b = (w[:, at[i]:at[i + 1]] for i in range(14))
    gate_cols = np.zeros((D, P), w.dtype)
    gate_cols[:, 0:8] = f_l
    gate_cols[:, 32:56] = g_n
    w1 = [A[n][0].reshape(2, 8, P, P).transpose(0, 2, 1, 3).reshape(2, P, D) for n in ("w1_ck", "w1_cv")]
    merge = np.stack([cols(g_a), cols(g_b)], 1).reshape(16, P, D)
    fox = np.stack([cols(q_f), cols(k_f)], 1).reshape(8, P, D)
    out["wmix"] = np.concatenate([cols(k_c), cols(v_c), cols(gate_cols), w1[0], merge, w1[1], cols(k_s), cols(k_w), cols(q_n),
                                  fox, cols(v_s), cols(v_w), cols(v_f)])
    out["pos"] = A["positions"][0]
    d = np.arange(P) % HD
    freq = np.float32(500000.0) ** (-np.arange(8, dtype=np.float32) / np.float32(8))
    out["rope_k"] = np.stack([np.where(d < 16, freq[d % 8], 0), np.where(d < 8, -1, np.where(d < 16, 1, 0))], 1).astype(np.float32)
    out["pe2"] = np.stack([A[n][0].reshape(16, P).T for n in ("pe_ck", "pe_cv")], 1)
    out["b_fg"] = np.repeat(A["b_forget"][0], 16)[:, None]
    out["w2"] = np.stack([np.concatenate([A[n][0]] * 2, 1) for n in ("w2_ck", "w2_cv")], 1)
    out["w_up"] = cols(np.concatenate([A["w_up_nsa"][0], A["w_up_fox"][0]]))
    out["w_o"] = A["w_o"][0].reshape(NT, P, D)
    out = {k: np.ascontiguousarray(v) for k, v in out.items()}
    for f in (1, 2):
        out[f"wg{f}"] = cols(A[f"w_gate{f}"][0])
        out[f"wu{f}"] = cols(A[f"w_up{f}"][0])
        out[f"wd{f}"] = A[f"w_down{f}"][0].reshape(NF, P, D)
    return out


def kernel(**inputs):
    import concourse.bacc as bacc
    import numpy as np
    from concourse.bass_utils import run_bass_kernel_spmd

    nc = bacc.Bacc("TRN2", target_bir_lowering=False, num_devices=1)
    arrays = {f"in_{k}": a for k, a in layout(inputs).items()}
    aps = {k[3:]: nc.dram_tensor(k, a.shape, mybir.dt.from_np(a.dtype), kind="ExternalInput").ap() for k, a in arrays.items()}
    out = nc.dram_tensor("outT", (NT, P, T), F32, kind="ExternalOutput").ap()
    build(nc, aps, {"outT": out})
    results = run_bass_kernel_spmd(nc, [arrays], core_ids=[0]).results[0]
    return np.ascontiguousarray(results["outT"].reshape(D, T).T).reshape(1, T, D)
```
